# Optimizing a Trainium2 kernel written in Bass

```python
import jax
import jax.numpy as jnp
from jax import lax
import numpy as np

D_MODEL = 1024
BATCH = 1
SEQ = 512
DEPTH = 1

HEAD_DIM = 64
FOX_HEADS = 6
NSA_HEADS = 4
MOBA_HEADS = 6
FOX_W = FOX_HEADS * HEAD_DIM
NSA_W = NSA_HEADS * HEAD_DIM
MOBA_W = MOBA_HEADS * HEAD_DIM
N_BRANCHES = 3

Q_BLOCK = 128
NSA_Q_BLOCK = 64
MOBA_Q_BLOCK = 32

NSA_CMP_LEN = 32
NSA_CMP_STRIDE = 16
NSA_CMP_HIDDEN = 256
NSA_SEL_LEN = 64
NSA_TOPN = 16
NSA_LOCAL = 2
NSA_WINDOW = 512

MOBA_BLOCK = 256
MOBA_TOPK = 3

N_GROUPS = 4
EXPERTS_PER_GROUP = 4
N_EXPERTS = N_GROUPS * EXPERTS_PER_GROUP
TOPK_IN_GROUP = 2
EXPERT_HIDDEN = 256

RMS_EPS = 1e-6
NEG_INF = -1e30
FORCE_SCORE = 1e9
FORGET_BIAS_SHIFT = 3.0

IN_SPLITS = (FOX_W, FOX_W, FOX_W, FOX_HEADS,
             NSA_W, HEAD_DIM, HEAD_DIM, HEAD_DIM, HEAD_DIM, HEAD_DIM, HEAD_DIM, N_BRANCHES * NSA_HEADS,
             MOBA_W, MOBA_W, MOBA_W,
             N_BRANCHES * D_MODEL)
IN_COLS = sum(IN_SPLITS)
FORGET_COL = 3 * FOX_W

kernel_name = 'hybrid_fox_nsa_moba_hmoe'

def _rmsnorm(x, g):
    xf = x.astype(jnp.float32)
    y = xf * lax.rsqrt(jnp.mean(xf * xf, axis=-1, keepdims=True) + RMS_EPS)
    return (y * g.astype(jnp.float32)).astype(x.dtype)

def _heads(t, n):
    b, s, _ = t.shape
    return t.reshape(b, s, n, HEAD_DIM).transpose(0, 2, 1, 3)

def _merge(o):
    b, h, s, d = o.shape
    return o.transpose(0, 2, 1, 3).reshape(b, s, h * d)

def _alibi_slopes(n):
    return jnp.asarray(2.0 ** (-8.0 * np.arange(1, n + 1) / n), dtype=jnp.float32)

def _masked_softmax(logits, mask):
    p = jax.nn.softmax(jnp.where(mask, logits, NEG_INF), axis=-1)
    return jnp.where(mask, p, 0.0)

def _fox_attention(q, k, v, forget_logit):
    b, h, s, d = q.shape
    nqb = s // Q_BLOCK
    scale = d ** -0.5
    c = jnp.cumsum(jax.nn.log_sigmoid(forget_logit.astype(jnp.float32)), axis=1).transpose(0, 2, 1)
    qb = q.reshape(b, h, nqb, Q_BLOCK, d).transpose(2, 0, 1, 3, 4)
    cb = c.reshape(b, h, nqb, Q_BLOCK).transpose(2, 0, 1, 3)
    key_pos = jnp.arange(s)

    def one_block(args):
        i, q_i, c_i = args
        t = i * Q_BLOCK + jnp.arange(Q_BLOCK)
        logits = jnp.einsum('bhqd,bhkd->bhqk', q_i, k).astype(jnp.float32) * scale
        logits = logits + c_i[..., :, None] - c[:, :, None, :]
        p = _masked_softmax(logits, key_pos[None, :] <= t[:, None])
        return jnp.einsum('bhqk,bhkd->bhqd', p.astype(v.dtype), v)

    o = lax.map(one_block, (jnp.arange(nqb), qb, cb))
    return o.transpose(1, 2, 0, 3, 4).reshape(b, h, s, d)

def _nsa_compress(kv, w1, b1, w2, pos):
    s = kv.shape[1]
    nc = (s - NSA_CMP_LEN) // NSA_CMP_STRIDE + 1
    idx = jnp.arange(nc)[:, None] * NSA_CMP_STRIDE + jnp.arange(NSA_CMP_LEN)[None, :]
    blocks = kv[:, idx, :] + pos
    hid = jax.nn.gelu(jnp.einsum('bnld,ldh->bnh', blocks, w1) + b1)
    return jnp.einsum('bnh,hd->bnd', hid, w2)

def _nsa_compressed_and_selected(q, k_cmp, v_cmp, k_sel, v_sel, slopes):
    b, h, s, d = q.shape
    scale = d ** -0.5
    nc = k_cmp.shape[1]
    n_sel = s // NSA_SEL_LEN
    topn = min(NSA_TOPN, n_sel)
    ratio = NSA_SEL_LEN // NSA_CMP_STRIDE
    span = NSA_CMP_LEN // NSA_CMP_STRIDE
    imp_len = ratio * n_sel + span - 1
    offsets = [m + n for m in range(ratio) for n in range(span)]
    cmp_end = jnp.arange(nc) * NSA_CMP_STRIDE + NSA_CMP_LEN - 1
    k_blk = k_sel.reshape(b, n_sel, NSA_SEL_LEN, d)
    v_blk = v_sel.reshape(b, n_sel, NSA_SEL_LEN, d)
    blk = jnp.arange(n_sel)
    b_idx = jnp.arange(b)[:, None, None]
    n_keys = topn * NSA_SEL_LEN
    nqb = s // NSA_Q_BLOCK
    qb = q.reshape(b, h, nqb, NSA_Q_BLOCK, d).transpose(2, 0, 1, 3, 4)

    def one_block(args):
        i, q_i = args
        t = i * NSA_Q_BLOCK + jnp.arange(NSA_Q_BLOCK)
        dist_c = t[:, None] - cmp_end[None, :]
        logits_c = (jnp.einsum('bhqd,bnd->bhqn', q_i, k_cmp).astype(jnp.float32) * scale
                    - slopes[:, None, None] * dist_c)
        p_c = _masked_softmax(logits_c, dist_c >= 0)
        o_c = jnp.einsum('bhqn,bnd->bhqd', p_c.astype(v_cmp.dtype), v_cmp)
        imp = jnp.pad(p_c.sum(axis=1), ((0, 0), (0, 0), (0, imp_len - nc)))
        imp_sel = sum(imp[..., o: o + ratio * n_sel: ratio] for o in offsets)
        cur = t // NSA_SEL_LEN
        causal = blk[None, :] <= cur[:, None]
        forced = (blk[None, :] == 0) | (blk[None, :] > cur[:, None] - NSA_LOCAL)
        score = jnp.where(causal, jnp.where(forced, FORCE_SCORE, imp_sel), -FORCE_SCORE)
        _, sel = lax.top_k(score, topn)
        k_g = k_blk[b_idx, sel].reshape(b, NSA_Q_BLOCK, n_keys, d)
        v_g = v_blk[b_idx, sel].reshape(b, NSA_Q_BLOCK, n_keys, d)
        key_pos = (sel[..., None] * NSA_SEL_LEN + jnp.arange(NSA_SEL_LEN)).reshape(b, NSA_Q_BLOCK, n_keys)
        dist_s = t[None, :, None] - key_pos
        logits_s = (jnp.einsum('bhqd,bqkd->bhqk', q_i, k_g).astype(jnp.float32) * scale
                    - slopes[None, :, None, None] * dist_s[:, None])
        p_s = _masked_softmax(logits_s, (dist_s >= 0)[:, None])
        o_s = jnp.einsum('bhqk,bqkd->bhqd', p_s.astype(v_g.dtype), v_g)
        return o_c, o_s

    o_c, o_s = lax.map(one_block, (jnp.arange(nqb), qb))
    o_c = o_c.transpose(1, 2, 0, 3, 4).reshape(b, h, s, d)
    o_s = o_s.transpose(1, 2, 0, 3, 4).reshape(b, h, s, d)
    return o_c, o_s

def _nsa_window(q, k, v, slopes):
    b, h, s, d = q.shape
    scale = d ** -0.5
    nqb = s // Q_BLOCK
    nprev = NSA_WINDOW // Q_BLOCK

    def band(t):
        tb = jnp.pad(t.reshape(b, nqb, Q_BLOCK, d), ((0, 0), (nprev, 0), (0, 0), (0, 0)))
        return jnp.concatenate([tb[:, j: j + nqb] for j in range(nprev + 1)], axis=2)

    k_band, v_band = band(k), band(v)
    q_pos = jnp.arange(nqb)[:, None] * Q_BLOCK + jnp.arange(Q_BLOCK)[None, :]
    key_pos = (jnp.arange(nqb)[:, None] - nprev) * Q_BLOCK + jnp.arange((nprev + 1) * Q_BLOCK)[None, :]
    diff = q_pos[:, :, None] - key_pos[:, None, :]
    mask = (diff >= 0) & (diff < NSA_WINDOW) & (key_pos[:, None, :] >= 0)
    qb = q.reshape(b, h, nqb, Q_BLOCK, d)
    logits = (jnp.einsum('bhnqd,bnkd->bhnqk', qb, k_band).astype(jnp.float32) * scale
              - slopes[:, None, None, None] * diff)
    p = _masked_softmax(logits, mask)
    o = jnp.einsum('bhnqk,bnkd->bhnqd', p.astype(v.dtype), v_band)
    return o.reshape(b, h, s, d)

def _moba_attention(q, k, v, slopes):
    b, h, s, d = q.shape
    scale = d ** -0.5
    nb = max(-(-s // MOBA_BLOCK), MOBA_TOPK + 1)
    pad = ((0, 0), (0, 0), (0, nb * MOBA_BLOCK - s), (0, 0))
    kp, vp = jnp.pad(k, pad), jnp.pad(v, pad)
    k_blk = kp.reshape(b, h, nb, MOBA_BLOCK, d)
    v_blk = vp.reshape(b, h, nb, MOBA_BLOCK, d)
    k_mean = k_blk.mean(axis=3)
    blk = jnp.arange(nb)
    b_idx = jnp.arange(b)[:, None, None, None]
    h_idx = jnp.arange(h)[None, :, None, None]
    n_keys = MOBA_TOPK * MOBA_BLOCK
    nqb = s // MOBA_Q_BLOCK
    qb = q.reshape(b, h, nqb, MOBA_Q_BLOCK, d).transpose(2, 0, 1, 3, 4)

    def one_block(args):
        i, q_i = args
        t = i * MOBA_Q_BLOCK + jnp.arange(MOBA_Q_BLOCK)
        cur = (i * MOBA_Q_BLOCK) // MOBA_BLOCK
        gate = jnp.einsum('bhqd,bhnd->bhqn', q_i, k_mean).astype(jnp.float32)
        gate = jnp.where(blk < cur, gate, -FORCE_SCORE)
        _, sel = lax.top_k(gate, MOBA_TOPK)
        k_g = k_blk[b_idx, h_idx, sel].reshape(b, h, MOBA_Q_BLOCK, n_keys, d)
        v_g = v_blk[b_idx, h_idx, sel].reshape(b, h, MOBA_Q_BLOCK, n_keys, d)
        key_pos = (sel[..., None] * MOBA_BLOCK + jnp.arange(MOBA_BLOCK)).reshape(b, h, MOBA_Q_BLOCK, n_keys)
        mask_past = jnp.repeat(sel < cur, MOBA_BLOCK, axis=-1)
        logits_past = (jnp.einsum('bhqd,bhqkd->bhqk', q_i, k_g).astype(jnp.float32) * scale
                       - slopes[None, :, None, None] * (t[None, None, :, None] - key_pos))
        own_k = lax.dynamic_slice_in_dim(kp, cur * MOBA_BLOCK, MOBA_BLOCK, axis=2)
        own_v = lax.dynamic_slice_in_dim(vp, cur * MOBA_BLOCK, MOBA_BLOCK, axis=2)
        dist_own = t[:, None] - (cur * MOBA_BLOCK + jnp.arange(MOBA_BLOCK))[None, :]
        logits_own = (jnp.einsum('bhqd,bhkd->bhqk', q_i, own_k).astype(jnp.float32) * scale
                      - slopes[:, None, None] * dist_own)
        mask_own = jnp.broadcast_to(dist_own >= 0, logits_own.shape)
        p = _masked_softmax(jnp.concatenate([logits_past, logits_own], axis=-1),
                            jnp.concatenate([mask_past, mask_own], axis=-1)).astype(v.dtype)
        return (jnp.einsum('bhqk,bhqkd->bhqd', p[..., :n_keys], v_g)
                + jnp.einsum('bhqk,bhkd->bhqd', p[..., n_keys:], own_v))

    o = lax.map(one_block, (jnp.arange(nqb), qb))
    return o.transpose(1, 2, 0, 3, 4).reshape(b, h, s, d)

def _token_mixers(h, w_in, b_in, cmp_w1, cmp_b1, cmp_w2, cmp_pos, w_br_fox, w_br_nsa, w_br_moba, w_out):
    b, s, _ = h.shape
    proj = jnp.einsum('bsd,dc->bsc', h, w_in) + b_in
    split_points = np.cumsum(IN_SPLITS)[:-1].tolist()
    (fq, fk, fv, f_forget, nq, kc, vc, ks, vs, kw, vw, n_gate,
     mq, mk, mv, merge_logit) = jnp.split(proj, split_points, axis=-1)
    o_fox = _fox_attention(_heads(fq, FOX_HEADS), _heads(fk, FOX_HEADS), _heads(fv, FOX_HEADS), f_forget)
    slopes_nsa = _alibi_slopes(NSA_HEADS)
    q_nsa = _heads(nq, NSA_HEADS)
    k_cmp = _nsa_compress(kc, cmp_w1[0], cmp_b1[0], cmp_w2[0], cmp_pos[0])
    v_cmp = _nsa_compress(vc, cmp_w1[1], cmp_b1[1], cmp_w2[1], cmp_pos[1])
    o_c, o_s = _nsa_compressed_and_selected(q_nsa, k_cmp, v_cmp, ks, vs, slopes_nsa)
    o_w = _nsa_window(q_nsa, kw, vw, slopes_nsa)
    g_nsa = jax.nn.sigmoid(n_gate.astype(jnp.float32)).reshape(b, s, N_BRANCHES, NSA_HEADS).transpose(2, 0, 3, 1)[..., None]
    o_nsa = (g_nsa[0] * o_c + g_nsa[1] * o_s + g_nsa[2] * o_w).astype(h.dtype)
    o_moba = _moba_attention(_heads(mq, MOBA_HEADS), _heads(mk, MOBA_HEADS), _heads(mv, MOBA_HEADS),
                             _alibi_slopes(MOBA_HEADS))
    y_fox = jnp.einsum('bsk,kd->bsd', _merge(o_fox), w_br_fox)
    y_nsa = jnp.einsum('bsk,kd->bsd', _merge(o_nsa), w_br_nsa)
    y_moba = jnp.einsum('bsk,kd->bsd', _merge(o_moba), w_br_moba)
    gate = jax.nn.sigmoid(merge_logit.astype(jnp.float32)).reshape(b, s, N_BRANCHES, D_MODEL)
    merged = (gate[:, :, 0] * y_fox + gate[:, :, 1] * y_nsa + gate[:, :, 2] * y_moba).astype(h.dtype)
    return jnp.einsum('bsd,de->bse', merged, w_out)

def _hier_moe(h, w_route_grp, b_route_grp, w_route_exp, b_route_exp, w_exp_gate, w_exp_up, w_exp_down):
    b, s, d = h.shape
    xt = h.reshape(b * s, d)
    grp_logits = (xt @ w_route_grp + b_route_grp).astype(jnp.float32)
    grp_prob = jax.nn.softmax(grp_logits, axis=-1)
    grp_weight = jax.nn.one_hot(jnp.argmax(grp_logits, axis=-1), N_GROUPS, dtype=jnp.float32) * grp_prob
    exp_logits = (xt @ w_route_exp + b_route_exp).astype(jnp.float32).reshape(-1, N_GROUPS, EXPERTS_PER_GROUP)
    exp_prob = jax.nn.softmax(exp_logits, axis=-1)
    top_p, top_i = lax.top_k(exp_prob, TOPK_IN_GROUP)
    top_p = top_p / top_p.sum(axis=-1, keepdims=True)
    within = jnp.sum(jax.nn.one_hot(top_i, EXPERTS_PER_GROUP, dtype=jnp.float32) * top_p[..., None], axis=-2)
    combine = grp_weight[:, :, None] * within
    out = jnp.zeros_like(xt)
    for g in range(N_GROUPS):
        e = slice(g * EXPERTS_PER_GROUP, (g + 1) * EXPERTS_PER_GROUP)
        a = jnp.einsum('td,edh->teh', xt, w_exp_gate[e])
        u = jnp.einsum('td,edh->teh', xt, w_exp_up[e])
        hid = (jax.nn.silu(a) * u * combine[:, g, :, None]).astype(xt.dtype)
        out = out + jnp.einsum('teh,ehd->td', hid, w_exp_down[e])
    return out.reshape(b, s, d)

def setup_inputs(seed: int = 0) -> dict:
    key = jax.random.key(seed)
    ks = jax.random.split(key, 21)
    f32 = jnp.float32
    L = DEPTH

    def nrm(k, shape, scale):
        return jax.random.normal(k, shape, f32) * scale

    b_in = nrm(ks[5], (L, IN_COLS), 0.02)
    b_in = b_in.at[:, FORGET_COL:FORGET_COL + FOX_HEADS].add(FORGET_BIAS_SHIFT)
    return {
        'x': nrm(ks[0], (BATCH, SEQ, D_MODEL), 1.0),
        'norm_mix_g': 1.0 + nrm(ks[1], (L, D_MODEL), 0.02),
        'norm_ffn_g': 1.0 + nrm(ks[2], (L, D_MODEL), 0.02),
        'final_norm_g': 1.0 + nrm(ks[3], (D_MODEL,), 0.02),
        'w_in': nrm(ks[4], (L, D_MODEL, IN_COLS), D_MODEL ** -0.5),
        'b_in': b_in,
        'cmp_w1': nrm(ks[6], (L, 2, NSA_CMP_LEN, HEAD_DIM, NSA_CMP_HIDDEN), (NSA_CMP_LEN * HEAD_DIM) ** -0.5),
        'cmp_b1': nrm(ks[7], (L, 2, NSA_CMP_HIDDEN), 0.02),
        'cmp_w2': nrm(ks[8], (L, 2, NSA_CMP_HIDDEN, HEAD_DIM), NSA_CMP_HIDDEN ** -0.5),
        'cmp_pos': nrm(ks[9], (L, 2, NSA_CMP_LEN, HEAD_DIM), 0.02),
        'w_br_fox': nrm(ks[10], (L, FOX_W, D_MODEL), FOX_W ** -0.5),
        'w_br_nsa': nrm(ks[11], (L, NSA_W, D_MODEL), NSA_W ** -0.5),
        'w_br_moba': nrm(ks[12], (L, MOBA_W, D_MODEL), MOBA_W ** -0.5),
        'w_out': nrm(ks[13], (L, D_MODEL, D_MODEL), D_MODEL ** -0.5),
        'w_route_grp': nrm(ks[14], (L, D_MODEL, N_GROUPS), D_MODEL ** -0.5),
        'b_route_grp': nrm(ks[15], (L, N_GROUPS), 0.01),
        'w_route_exp': nrm(ks[16], (L, D_MODEL, N_EXPERTS), D_MODEL ** -0.5),
        'b_route_exp': nrm(ks[17], (L, N_EXPERTS), 0.01),
        'w_exp_gate': nrm(ks[18], (L, N_EXPERTS, D_MODEL, EXPERT_HIDDEN), D_MODEL ** -0.5),
        'w_exp_up': nrm(ks[19], (L, N_EXPERTS, D_MODEL, EXPERT_HIDDEN), D_MODEL ** -0.5),
        'w_exp_down': nrm(ks[20], (L, N_EXPERTS, EXPERT_HIDDEN, D_MODEL), EXPERT_HIDDEN ** -0.5),
    }

def reference(x, norm_mix_g, norm_ffn_g, final_norm_g, w_in, b_in, cmp_w1, cmp_b1, cmp_w2, cmp_pos,
              w_br_fox, w_br_nsa, w_br_moba, w_out, w_route_grp, b_route_grp, w_route_exp, b_route_exp,
              w_exp_gate, w_exp_up, w_exp_down):
    for l in range(DEPTH):
        h = _rmsnorm(x, norm_mix_g[l])
        x = x + _token_mixers(h, w_in[l], b_in[l], cmp_w1[l], cmp_b1[l], cmp_w2[l], cmp_pos[l],
                              w_br_fox[l], w_br_nsa[l], w_br_moba[l], w_out[l])
        h = _rmsnorm(x, norm_ffn_g[l])
        x = x + _hier_moe(h, w_route_grp[l], b_route_grp[l], w_route_exp[l], b_route_exp[l],
                          w_exp_gate[l], w_exp_up[l], w_exp_down[l])
    return _rmsnorm(x, final_norm_g)


_drawn_inputs = setup_inputs


def setup_inputs(seed=0):
    import zlib

    import numpy as np

    out = dict(_drawn_inputs(seed))
    spreads = {}
    factors = {'norm_mix_g': 2.755,
     'final_norm_g': 9.002,
     'cmp_b1': 19.604,
     'cmp_pos': 19.351,
     'b_route_grp': 59.992,
     'b_route_exp': 25.616,
     'norm_ffn_g': 5.366}
    for name, (base, spread) in spreads.items():
        noise = np.random.default_rng([zlib.crc32(name.encode()), seed]).standard_normal(out[name].shape)
        drawn = base * np.exp(spread * noise) if base else spread * noise
        out[name] = jnp.asarray(drawn.astype(out[name].dtype))
    for name, factor in factors.items():
        out[name] = (out[name] * factor).astype(out[name].dtype)
    return out
```

```python
from contextlib import ExitStack

import concourse.bass as bass
from concourse import mybir

F32 = mybir.dt.float32
F32R = mybir.dt.float32r
BF16 = mybir.dt.bfloat16
I32 = mybir.dt.int32
ALU = mybir.AluOpType
ACT = mybir.ActivationFunctionType
AX_X = mybir.AxisListType.X

P = 128
S = 512
D = 1024
KC = D // P
NB = S // P
HD = 64
FOX_H, NSA_H, MOBA_H = 6, 4, 6
NF = 3 * FOX_H * HD
C_FORGET = NF
C_NSA = C_FORGET + FOX_H
C_GATE = C_NSA + NSA_H * HD + 6 * HD
C_MOBA = C_GATE + 3 * NSA_H
C_MERGE = C_MOBA + 3 * MOBA_H * HD
CMP_LEN, CMP_STRIDE, CMP_HID = 32, 16, 256
NCMP = (S - CMP_LEN) // CMP_STRIDE + 1
MOBA_BLOCK = 256
NE, NG, EPG = 16, 4, 4
EH = 256
NOV = (2 * S - NE) // P
SLOTS = (NE + NOV) * P
BIG = 1e30
INVALID_SCORE = -1e9
EPS = 1e-6
QSCALE = -(HD ** -0.5)
NSA_SLOPES = [2.0 ** (-8.0 * (h + 1) / NSA_H) for h in range(NSA_H)]
MOBA_SLOPES = [2.0 ** (-8.0 * (h + 1) / MOBA_H) for h in range(MOBA_H)]
NRAW, NSPLIT = 3, 3
IN_FLIGHT = 2
MRAW, MSPLIT = 12, 4
NPROB, NPROBT, NSUM = 3, 3, 6
TR_LAG, PV_LAG = 2, 4
BR_CHUNKS = (3, 2, 3)

R_NORM, R_B1, R_POS = 48, 56, 60
R_FFN = R_POS + 2 * CMP_LEN // 2
R_ALL = R_FFN + KC
R_GATE = 24


def weight_stream():
    loads, pieces = [], []

    def tile(kind, j, c):
        return kind, j, [(c, P)]

    def load_pair(pair):
        loads.append(("in", [run for t in pair for run in t[2]]))
        for half, (kind, j, runs) in enumerate(pair):
            pieces.append(dict(load=len(loads) - 1, half=half, kind=kind, j=j, k=KC, n=sum(w for _, w in runs)))

    tiles = [tile(k, j, 384 * n + P * j) for n, k in enumerate(("fq", "fk", "fv")) for j in range(3)]
    tiles += [("sm", 0, [(C_FORGET, FOX_H), (C_GATE, 3 * NSA_H)])]
    tiles += [tile("nq", j, C_NSA + P * j) for j in range(2)]
    tiles += [tile(k, 0, C_NSA + 256 + P * n) for n, k in enumerate(("cc", "ss", "sw"))]
    tiles += [tile(k, j, C_MOBA + 384 * n + P * j) for n, k in enumerate(("mq", "mk", "mv")) for j in range(3)]
    for n in range(0, len(tiles), 2):
        load_pair(tiles[n:n + 2])
    for b in range(3):
        for dp in range(KC // 2):
            load_pair([tile("g", KC * b + d, C_MERGE + D * b + P * d) for d in (2 * dp, 2 * dp + 1)])
            if dp % 2 == 0:
                loads.append(("br", (b, dp // 2)))
                br_load = len(loads) - 1
            pieces.append(dict(load=br_load, half=dp % 2, kind="y", j=4 * b + dp, k=BR_CHUNKS[b], n=256))
    for n in range(4):
        loads.append(("out", (n // 2, n % 2)))
        for half in range(2):
            pieces.append(dict(load=len(loads) - 1, half=half, kind="o", j=2 * n + half, k=2, n=512))
    return loads, pieces


def column_runs(runs):
    out, at = [], 0
    for c, w in runs:
        if out and out[-1][1] + out[-1][2] == c:
            out[-1][2] += w
        else:
            out.append([at, c, w])
        at += w
    return out


def attention_units():
    units = [("f", h, i) for h in range(FOX_H) for i in range(NB)]
    units += [(k, h, i) for h in range(NSA_H) for k in "sw" for i in range(NB)]
    return units + [("m", h, i) for h in range(MOBA_H) for i in range(NB)]


def mixer_order(pieces, units):
    seq, split, tiles = [("COLS", 0)], 0, 0
    n_fox_tiles = 12
    n_units, n_fox = len(units), FOX_H * NB

    after_tile, after_unit = [], []

    def split_to(end):
        nonlocal split
        while split < min(end, len(pieces)):
            seq.append(("H", split))
            split += 1

    def tile(p):
        nonlocal tiles
        split_to(tiles + NSPLIT)
        tiles += 1
        kind = pieces[p]["kind"]
        if kind == "o" and pieces[p]["j"] == 0:
            seq.append(("M", 0))
        seq.append(("T", p))
        if kind == "o" and pieces[p]["j"] == 3:
            seq.append(("XA", 0))
        if kind == "o" and pieces[p]["j"] == 5:
            seq.extend(("RT", k) for k in range(KC // 2))
        if kind == "o" and pieces[p]["j"] == 7:
            seq.append(("XA", 1))
            seq.extend(("RT", k) for k in range(KC // 2, KC))
        flush(after_tile)
        if kind in ("fv", "mv", "ss", "sw"):
            after_tile.append(("VT", p))
        if kind == "sm":
            after_tile.append(("SM", p))
        if kind == "mk":
            after_tile.append(("KS", pieces[p]["j"]))

    def flush(items):
        seq.extend(items)
        items.clear()

    def finish(u):
        seq.append(("PV", u))
        flush(after_unit)
        kind, h, i = units[u]
        if h % 2 == 1 and i == NB - 1 and kind in "fwm":
            after_unit.append(("OT", ("fwm".index(kind), h // 2)))

    def unit(u, first):
        seq.append(("QK", u))
        if u - TR_LAG >= first:
            seq.append(("TR", u - TR_LAG))
        if u - PV_LAG >= first:
            finish(u - PV_LAG)

    def drain(end):
        for u in range(end - TR_LAG, end):
            seq.append(("TR", u))
            finish(u - PV_LAG + TR_LAG)
        for u in range(end - PV_LAG + TR_LAG, end):
            finish(u)
        flush(after_unit)

    for k in range(KC):
        seq.append(("XT", k))
        if k == KC // 2 - 1:
            split_to(1)
    first = list(range(n_fox_tiles))
    sm = [pc["kind"] for pc in pieces].index("sm")
    first[sm - 1], first[sm] = sm, sm - 1
    for p in first:
        tile(p)
    flush(after_tile)
    p = n_fox_tiles
    for u in range(n_fox):
        unit(u, 0)
        if u % 6 == 2 and pieces[p]["kind"][0] != "m":
            tile(p)
            p += 1
    drain(n_fox)
    while pieces[p]["kind"][0] != "m":
        tile(p)
        p += 1
    for stage in ("CB", "CH0", "CH1", "CX", "CK", "CS", "CT", "CO"):
        seq.append((stage, 0))
        if stage != "CO":
            tile(p)
            p += 1
    flush(after_tile)
    first, fill = p, len(pieces) - 8 - 12 - p
    for n, u in enumerate(range(n_fox, n_units)):
        unit(u, n_fox)
        while p < first + (n + 1) * fill // (n_units - n_fox):
            tile(p)
            p += 1
    drain(n_units)
    while p < len(pieces):
        tile(p)
        p += 1
    return seq


def build(nc, x, norm_mix_g, norm_ffn_g, final_norm_g, w_in, b_in, cmp_w1, cmp_b1, cmp_w2, cmp_pos,
          w_br_fox, w_br_nsa, w_br_moba, w_out, w_route_grp, b_route_grp, w_route_exp, b_route_exp,
          w_exp_gate, w_exp_up, w_exp_down, out):
    loads, pieces = weight_stream()
    units = attention_units()
    seq = mixer_order(pieces, units)
    n_pieces, n_units, n_fox = len(pieces), len(units), FOX_H * NB

    proj_use, tp_use, o_use, sc_use = {}, {}, {}, {}
    for it in seq:
        kind, a = it
        if kind == "T" and pieces[a]["kind"] != "o":
            for d in range(2 if pieces[a]["kind"] == "y" else 1):
                proj_use[(a, d)] = len(proj_use)
        if kind in ("COLS", "XT", "VT", "SM", "TR", "OT", "CX", "CT"):
            tp_use[it] = len(tp_use)
        if kind in ("PV", "KS", "CH0", "CH1", "CK"):
            o_use[it] = len(o_use)
        if kind == "CO":
            for i in range(NB):
                o_use[("CO", i)] = len(o_use)
        if kind in ("QK", "CS"):
            sc_use[it] = len(sc_use)

    def proj_who(key):
        return "dve" if pieces[key[0]]["kind"] in ("fq", "nq", "mq", "sm", "y") else "act"

    def tp_who(it):
        if it[0] == "TR":
            return "act" if units[it[1]][2] in (0, 2) else "dve"
        return "act" if it[0] in ("CT", "COLS") else "dve"

    def o_who(it):
        return "act" if it[0] in ("CH0", "CH1") else "dve"

    def emptied(uses, who):
        n, at = {"act": 0, "dve": 0}, {}
        for it in uses:
            n[who(it)] += 1
            at[it] = (who(it), n[who(it)])
        return at

    proj_free, tp_free, o_free = emptied(proj_use, proj_who), emptied(tp_use, tp_who), emptied(o_use, o_who)
    at_proj, at_tp, at_o, at_sc = list(proj_use), list(tp_use), list(o_use), list(sc_use)
    piece_of = {(pc["kind"], pc["j"]): q for q, pc in enumerate(pieces)}
    last_piece_of = {pc["load"]: q for q, pc in enumerate(pieces)}
    v_tiles = [it[1] for it in seq if it[0] == "VT"]
    order = {it: n for n, it in enumerate(seq)}
    for b in range(3):
        assert all(order[("OT", (b, j))] < order[("T", piece_of[("y", 4 * b)])] for j in range(BR_CHUNKS[b]))
    assert order[("OT", (2, 0))] > order[("T", piece_of[("y", 3)])] > order[("CO", 0)]

    stream = []
    for it in seq:
        if it[0] == "H" and ("w", pieces[it[1]]["load"]) not in stream:
            stream.append(("w", pieces[it[1]]["load"]))
        elif it[0] in ("CH0", "CH1"):
            stream += [("c", 2 * int(it[0][2])), ("c", 2 * int(it[0][2]) + 1)]
    place = {ld: n for n, ld in enumerate(stream)}

    def slot(ld):
        return place[ld] % NRAW

    landings, so_far = {}, [0] * NRAW
    for ld in stream:
        several = ld[0] == "w" and loads[ld[1]][0] == "in"
        so_far[slot(ld)] += 16 * (len(column_runs(loads[ld[1]][1])) if several else 1)
        landings[ld] = so_far[slot(ld)]

    master_heads = [("s", h) for h in range(NSA_H)] + [("m", h) for h in range(MOBA_H)]
    master_end = [1 + max(u for u, (kk, hh, _) in enumerate(units) if hh == h and kk in ("sw" if k == "s" else "m"))
                  for k, h in master_heads]
    master_from = [1, n_fox] + master_end[:-2]
    N_MASTER0 = 5 + NSA_H

    with ExitStack() as ctx:
        def sem(name):
            return ctx.enter_context(nc.semaphore(name))

        def sb(where, name, shape, dt=F32):
            return where.enter_context(nc.sbuf_tensor(name, shape, dt))

        def dram(name, shape, dt):
            return nc.dram_tensor(name, shape, dt, kind="Internal").ap()

        bank = [ctx.enter_context(nc.psum_tensor(f"bank{i}", [P, 512], F32)) for i in range(8)]
        proj_bank, sc_bank, tp_bank, o_bank = bank[0:2], bank[2:4], bank[4:6], bank[6:8]

        h2_dram = dram("h2_dram", (S, D), F32)
        y_dram = dram("y_dram", (SLOTS, D), F32)

        ident = sb(ctx, "ident", [P, P])
        zeros = sb(ctx, "zeros", [P, S])
        raw = sb(ctx, "raw", [P, NRAW, 2048])
        w_rt = sb(ctx, "w_rt", [P, KC, NG + NE])
        b_rt = sb(ctx, "b_rt", [P, NG + NE])
        gcol = sb(ctx, "gcol", [P, KC])

        mix = ExitStack()
        hT_hi = sb(mix, "hT_hi", [P, KC, S], F32R)
        hT_lo = sb(mix, "hT_lo", [P, KC, S], F32R)
        w_hi = sb(mix, "w_hi", [P, NSPLIT, 1024], F32R)
        w_lo = sb(mix, "w_lo", [P, NSPLIT, 1024], F32R)
        xm = sb(mix, "xm", [P, NB * D])
        qT = sb(mix, "qT", [P, 3, S])
        kT = sb(mix, "kT", [P, 6, S])
        nqT = sb(mix, "nqT", [P, 2, S])
        nkT = sb(mix, "nkT", [P, 4, S])
        v_sb = sb(mix, "v_sb", [P, NB, 384])
        nv_sb = sb(mix, "nv_sb", [P, 2, NB, HD])
        dist = sb(mix, "dist", [P, S])
        master = sb(mix, "master", [P, 2, S])
        foxmask = master[:, 1, :]
        prob = sb(mix, "prob", [P, NPROB, S])
        probT = sb(mix, "probT", [P, NPROBT, S])
        oT_hi = sb(mix, "oT_hi", [P, 5, S], F32R)
        oT_lo = sb(mix, "oT_lo", [P, 5, S], F32R)
        obuf = sb(mix, "obuf", [P, 2, NB, P])
        onsa = sb(mix, "onsa", [P, NB, 2 * P])
        shared = sb(mix, "shared", [P, 4, S])
        vstage = sb(mix, "vstage", [P, 2, S])
        rows = sb(mix, "rows", [P, P])
        cols = sb(mix, "cols", [P, R_ALL])
        halfb = sb(mix, "halfb", [P, 3 * KC])
        sel_head = sb(mix, "sel_head", [P, FOX_H, P], BF16)
        sel_row = sb(mix, "sel_row", [P, 2, MOBA_BLOCK], BF16)
        penalty = sb(mix, "penalty", [P, 3, MOBA_BLOCK], BF16)
        csplit = sb(mix, "csplit", [P, S], BF16)
        cmid = sb(mix, "cmid", [FOX_H, S], BF16)
        sm_sb = onsa[0:FOX_H + 3 * NSA_H, 0:2, :].rearrange("p a b -> p (a b)")
        gates = sb(mix, "gates", [P, NB, 3 * NSA_H])
        ksum = sb(mix, "ksum", [P, 3, 2])
        w2c = sb(mix, "w2c", [P, 4, HD])
        hidc = sb(mix, "hidc", [P, 4, 32])
        hidn = prob[0:NCMP, 0, :].rearrange("p (a h) -> p a h", a=2)
        kcp = sb(mix, "kcp", [P, 2, 32])
        vbd = sb(mix, "vbd", [P, NSA_H * HD])
        cstat = sb(mix, "cstat", [P, 4, 16])
        valid = sb(mix, "valid", [P, 16])
        stat = sb(mix, "stat", [P, 5, NB])
        negmax = sb(mix, "negmax", [P, 4])
        rowsum = sb(mix, "rowsum", [P, NSUM])
        rinv = sb(mix, "rinv", [P, 2])
        coef = sb(mix, "coef", [P, 2])
        mix.close()
        x_sb = xm[:, :].rearrange("p (b d) -> p b d", b=NB)
        m_sb = xm[:, :].rearrange("p (k t) -> p k t", k=KC)
        cmp_mask = m_sb[:, 0, :]
        kc2, vc2, probc, pcT = shared[:, 0, :], shared[:, 1, :], shared[:, 0, :], shared[:, 1, :]
        cblk = shared[:, 2:4, :].rearrange("p a (c n) -> p (a c) n", n=32)

        ffn = ExitStack()
        m_hi = sb(ffn, "m_hi", [P, MSPLIT, 1024], F32R)
        m_lo = sb(ffn, "m_lo", [P, MSPLIT, 1024], F32R)
        assert 2 * MSPLIT * 1024 == 2 * KC * S and 2 * NSPLIT * 1024 == NRAW * 2048
        raw_b = sb(ffn, "raw_b", [P, NRAW, 2048])
        x1 = sb(ffn, "x1", [P, NB, D])
        raw_c = sb(ffn, "raw_c", [P, NRAW, 2048])
        h2 = raw_c[:, 0:2, :].rearrange("p a (b d) -> p (a b) d", d=D)
        h2T = raw_c[:, 2, :].rearrange("p (b d) -> p b d", d=D)
        gffn = sb(ffn, "gffn", [P, D])
        gfin = sb(ffn, "gfin", [P, D])
        raw_a = sb(ffn, "raw_a", [P, NRAW, 2048])
        xg = sb(ffn, "xg", [P, 2, D])
        xT_hi = sb(ffn, "xT_hi", [P, 2, KC, P], F32R)
        xT_lo = sb(ffn, "xT_lo", [P, 2, KC, P], F32R)
        sil = sb(ffn, "sil", [P, 2, EH])
        hid = sb(ffn, "hid", [P, 2, EH])
        hidT_hi = sb(ffn, "hidT_hi", [P, 2, 2, P], F32R)
        hidT_lo = sb(ffn, "hidT_lo", [P, 2, 2, P], F32R)
        y_sb = sb(ffn, "y_sb", [P, 2, D])
        tri = sb(ffn, "tri", [P, P], BF16)
        ones = sb(ffn, "ones", [P, P], BF16)
        selb = sb(ffn, "selb", [P, NB * NE], BF16)
        lgT = sb(ffn, "lgT", [NG + NE, S])
        fstat = sb(ffn, "fstat", [P, 9, NB])
        lg = sb(ffn, "lg", [P, NB, NG + NE])
        rt = sb(ffn, "rt", [P, 12, NB * NE])
        rg = sb(ffn, "rg", [P, 9, NB * NG])
        rw = sb(ffn, "rw", [P, 12, NB])
        prio = sb(ffn, "prio", [P, NB * NE])
        eoff = sb(ffn, "eoff", [P, NE])
        tokid = sb(ffn, "tokid", [P, 2, NB])
        jtile = sb(ffn, "jtile", [P, NOV * NE])
        ecnt = sb(ffn, "ecnt", [P, 6, NE])
        ovmap = sb(ffn, "ovmap", [P, NOV * NE])
        ovcnt = sb(ffn, "ovcnt", [P, NOV + 1])
        ovint = sb(ffn, "ovint", [P, NOV + 1], I32)
        slot_i = sb(ffn, "slot_i", [P, 2, NB], I32)
        lane = sb(ffn, "lane", [P, P])
        edge = sb(ffn, "edge", [P, NE + NOV + 1])
        atleast = sb(ffn, "atleast", [P, 2 * NB, NE + NOV + 1])
        in_tile = sb(ffn, "in_tile", [P, 2 * NB, NE + NOV])
        part_id = sb(ffn, "part_id", [P, 2, 2 * NB, NE + NOV], BF16)
        tiles = sb(ffn, "tiles", [P, 2, 2 * NB])
        ids = sb(ffn, "ids", [P, NE + NOV], I32)
        ov_id = sb(ffn, "ov_id", [P, 1], I32)
        iot = sb(ffn, "iot", [P, P], I32)
        ffn.close()
        in_lane = y_sb[:, 0, 0:D // 2].bitcast(BF16).rearrange("p (n t) -> p n t", t=P)
        xT = h2T[:, :, :].rearrange("p a (b t) -> p (a b) t", t=S)
        mraw = [t[:, n, :] for t in (raw, raw_a, raw_b, raw_c) for n in range(NRAW)]

        x_in = [sem(f"x_in{i}") for i in range(NB)]
        w_landed = [sem(f"w_landed{i}") for i in range(NRAW)]
        (rows_zero, rows_in, small_in, filled, zeroed, const_ready, master_ready, cw_used, hi_done, lo_done,
         proj_done, proj_act, proj_dve, tp_done, tp_act, tp_dve, tp_hi, sc_done, shifted, exp_done, o_done,
         o_act, o_dve, sq_done, std_done, var_ready, x_scaled, bias_halved, abs_ready, sm_act, sm_gates,
         gates_ready, c_ready, ksum_ready, cblk_ready, c_shifted, c_centered, c_exp, merged, m_hi_done,
         m_split, out_mm, out_blocks, link_dve) = [sem(n) for n in (
             "rows_zero rows_in small_in filled zeroed const_ready master_ready cw_used hi_done lo_done "
             "proj_done proj_act proj_dve tp_done tp_act tp_dve tp_hi sc_done shifted exp_done o_done "
             "o_act o_dve sq_done std_done var_ready x_scaled bias_halved abs_ready sm_act sm_gates "
             "gates_ready c_ready ksum_ready cblk_ready c_shifted c_centered c_exp merged m_hi_done "
             "m_split out_mm out_blocks link_dve").split()]
        (x_again, g_in, x1_ready, fsq_done, fvar_ready, fstd_done, root_ready, gained, h2_ready, h2_out, rtp_done,
         rt_act, rt_dve, lgT_ready, lgT_done,
         logits_mm, lg_centered, lg_exp, sel_ready, pos_mm, onehot_ready, ids_mm, ids_ready, ov_ready,
         fconst, e_hi, e_lo, e_used, e_tp, e_tp_hi, e_tp_free, sil_done, hid_done, y_done, acc_done,
         nsq_done, nvar_ready, nstd_done, fin_ready, out_done) = [sem(n) for n in (
             "x_again g_in x1_ready fsq_done fvar_ready fstd_done root_ready gained h2_ready h2_out rtp_done "
             "rt_act rt_dve lgT_ready lgT_done "
             "logits_mm lg_centered lg_exp sel_ready pos_mm onehot_ready ids_mm ids_ready ov_ready "
             "fconst e_hi e_lo e_used e_tp e_tp_hi e_tp_free sil_done hid_done y_done acc_done "
             "nsq_done nvar_ready nstd_done fin_ready out_done").split()]
        (v_in, v_id, v_gath, v_tp, v_xT, v_gu, v_sil, v_hid, v_htp, v_hT, v_y, v_ev, v_out) = [sem(n) for n in (
            "v_in v_id v_gath v_tp v_xT v_gu v_sil v_hid v_htp v_hT v_y v_ev v_out").split()]
        e_landed = [sem(f"e_landed{i}") for i in range(MRAW)]
        xg_in = [sem(f"xg_in{i}") for i in range(2)]
        y_out = [sem(f"y_out{i}") for i in range(2)]
        back_in = [sem(f"back_in{i}") for i in range(NB)]

        w_in_v = w_in[0].rearrange("(k p) n -> p k n", p=P)
        w_br_v = [w[0].rearrange("(k p) n -> p k n", p=P) for w in (w_br_fox, w_br_nsa, w_br_moba)]
        w_out_v = w_out[0].rearrange("(k p) n -> p k n", p=P)
        x_v = x[0].rearrange("(b p) d -> b p d", p=P)
        out_v = out[0].rearrange("(b p) d -> b p d", p=P)

        def slot_tile(ld, n):
            return raw[:, slot(ld), :].rearrange("p (k n) -> p k n", n=n)

        def piece_raw(p):
            pc = pieces[p]
            h, ld = pc["half"], ("w", pc["load"])
            if pc["kind"] == "y":
                return slot_tile(ld, 512)[:, 0:pc["k"], 256 * h:256 * h + 256]
            if pc["kind"] == "o":
                return slot_tile(ld, 512)[:, 2 * h:2 * h + 2, :]
            return slot_tile(ld, 256)[:, :, P * h:P * h + pc["n"]]

        def piece_split(part, p):
            pc = pieces[p]
            return part[:, p % NSPLIT, 0:pc["k"] * pc["n"]].rearrange("p (k n) -> p k n", n=pc["n"])

        def wait_emptied(eng, counts, key, act_sem, dve_sem):
            who, n = counts[key]
            eng.wait_ge(act_sem if who == "act" else dve_sem, n)

        def wait_piece_used(eng, p):
            if pieces[p]["kind"] == "o" and pieces[p]["j"] % 4 == 3:
                eng.wait_ge(out_blocks, NB * (pieces[p]["j"] // 4 + 1))
            elif pieces[p]["kind"] == "o":
                eng.wait_ge(out_mm, pieces[p]["j"] - pieces[p]["j"] // 4 + 1)
            else:
                eng.wait_ge(proj_done, proj_use[(p, 1 if pieces[p]["kind"] == "y" else 0)] + 1)

        def wait_tp_emptied(eng, it):
            wait_emptied(eng, tp_free, it, tp_act, tp_dve)

        def wait_proj_emptied(eng, kind, j, d=0):
            wait_emptied(eng, proj_free, (piece_of[(kind, j)], d), proj_act, proj_dve)

        def xt_bank(k):
            return bank[(5, 6, 7, 2, 3, 4)[k % 6]]

        def o_chunk(b, pair):
            return 3 + pair if b == 1 else pair

        def unit_width(u):
            return P * (units[u][2] + 1)

        def nsa_coef_gate(u):
            kind, h, _ = units[u]
            return (NSA_H if kind == "s" else 2 * NSA_H) + h

        fox_values_used = o_use[("PV", n_fox - 1)] + 1

        def expert(r, i):
            return r + 4 * i

        def pc_no(r, i, k):
            return k if r == 0 else 6 * r - 2 + k + 24 * i

        def pc_mod(r, k):
            return k if r == 0 else 6 * r - 2 + k

        def rounds(eng, opening, one_round):
            opening()
            for r in range(1, 5):
                one_round(r, 0)
            with eng.Fori(1, NE // 4 - 1) as i:
                for r in range(1, 5):
                    one_round(r, i)
            for r in range(1, 4):
                one_round(r, NE // 4 - 1)

        def is_last(r, i):
            return r == 3 and isinstance(i, int) and i == NE // 4 - 1

        def not_before_2(r, i):
            return r >= 2 or not isinstance(i, int) or expert(r, i) >= 2

        def rows_use(r, i):
            return 0 if r == 0 and isinstance(i, int) and i == 0 else 3 * r - 1 + 12 * i

        def hidden_use(r, i):
            return 3 * NE - 1 if is_last(r, i) else 3 * r + 4 + 12 * i

        def use_bank(n0):
            return tp_bank[n0 % 2]

        def y_bank(r, half):
            return bank[(2 if r % 2 == 0 else 6) + half]

        def four(ap):
            return ap[:, :].rearrange("p (c t) -> p c t", c=4)

        def two(ap):
            return ap[:, 0:2 * P].rearrange("p (c t) -> p c t", c=2)

        def gathered(i, c):
            if i == 0:
                return xg[:, c, :]
            return raw_a[:, i - 1, D * c:D * c + D]

        block = ctx.enter_context(nc.Block())

        @block.sync
        def _(sp):
            def small_loads():
                sp.dma_start(w2c[:, :, :], cmp_w2[0].rearrange("a (k p) d -> p (a k) d", p=P)).then_inc(small_in, 16)
                sp.dma_start(w_rt[:, :, 0:NG], w_route_grp[0].rearrange("(k p) n -> p k n", p=P),
                              allow_slow_non_contiguous=True).then_inc(small_in, 16)
                sp.dma_start(w_rt[:, :, NG:NG + NE], w_route_exp[0].rearrange("(k p) n -> p k n", p=P),
                              allow_slow_non_contiguous=True).then_inc(small_in, 16)
                sp.dma_start(b_rt[:, 0:NG], b_route_grp[0].partition_broadcast(P)).then_inc(small_in, 16)
                sp.dma_start(b_rt[:, NG:NG + NE], b_route_exp[0].partition_broadcast(P)).then_inc(small_in, 16)

            for i in range(NB):
                sp.dma_start(x_sb[:, i, :], x_v[i]).then_inc(x_in[i], 16)
            sp.wait_ge(rows_zero, 1)
            for r0, r1, src in (
                    (0, 9, b_in[0, 0:NF].rearrange("(t p) -> t p", p=P)),
                    (10, 15, b_in[0, C_NSA:C_GATE].rearrange("(t p) -> t p", p=P)),
                    (15, R_NORM, b_in[0, C_MOBA:C_MERGE + 3 * D].rearrange("(t p) -> t p", p=P)),
                    (R_NORM, R_B1, norm_mix_g[0].rearrange("(t p) -> t p", p=P)),
                    (R_B1, R_POS, cmp_b1[0].rearrange("a (t p) -> (a t) p", p=P)),
                    (R_POS, R_FFN, cmp_pos[0].rearrange("a (c l) d -> (a c) (l d)", l=2)),
                    (R_FFN, R_ALL, norm_ffn_g[0].rearrange("(t p) -> t p", p=P))):
                sp.dma_start(rows[r0:r1, :], src).then_inc(rows_in, 16)
            sp.dma_start(rows[9:10, 0:FOX_H], b_in[0:1, C_FORGET:C_NSA]).then_inc(rows_in, 16)
            sp.dma_start(rows[9:10, FOX_H:FOX_H + 12], b_in[0:1, C_GATE:C_MOBA]).then_inc(rows_in, 16)
            for n, ld in enumerate(stream):
                if n == NRAW:
                    small_loads()
                if n >= NRAW:
                    kind, a = stream[n - NRAW]
                    if kind == "c" and a % 2 == 0:
                        sp.wait_ge(cw_used, a // 2 + 1)
                    elif kind == "c":
                        sp.wait_ge(o_done, o_use[(f"CH{a // 2}", 0)] + 1)
                    else:
                        sp.wait_ge(lo_done, last_piece_of[a] + 1)
                kind, a = ld
                landed = w_landed[slot(ld)]
                if kind == "c":
                    src = cmp_w1[0, a // 2].rearrange("(c l) d h -> (l d) c h", l=2)
                    c0 = 8 * (a % 2)
                    sp.dma_start(slot_tile(ld, CMP_HID), src[:, c0:c0 + 8, :]).then_inc(landed, 16)
                    continue
                what, arg = loads[a]
                if what == "in":
                    for at, c, w in column_runs(arg):
                        sp.dma_start(slot_tile(ld, 256)[:, :, at:at + w], w_in_v[:, :, c:c + w],
                                     allow_slow_non_contiguous=True).then_inc(landed, 16)
                elif what == "br":
                    b, half = arg
                    sp.dma_start(slot_tile(ld, 512)[:, 0:BR_CHUNKS[b], :],
                                 w_br_v[b][:, :, 512 * half:512 * half + 512]).then_inc(landed, 16)
                else:
                    half, kq = arg
                    sp.dma_start(slot_tile(ld, 512), w_out_v[:, 4 * kq:4 * kq + 4, 512 * half:512 * half + 512]
                                 ).then_inc(landed, 16)
            sp.wait_ge(m_split, KC)
            for i in range(NB):
                sp.dma_start(x1[:, i, :], x_v[i]).then_inc(x_again, 16)
            sp.dma_start(gffn[:, :], norm_ffn_g[0].partition_broadcast(P)).then_inc(g_in, 16)
            sp.dma_start(gfin[:, :], final_norm_g.partition_broadcast(P)).then_inc(g_in, 16)

            def gate_up(e, half, n):
                dst = mraw[n].rearrange("p (k n) -> p k n", n=2 * EH)
                for j, w in enumerate((w_exp_gate, w_exp_up)):
                    src = w[0, bass.ds(e, 1)].rearrange("a (k p) n -> p (a k) n", p=P)
                    sp.dma_start(dst[:, :, EH * j:EH * j + EH], src[:, 4 * half:4 * half + 4, :]
                                 ).then_inc(e_landed[n], 16)

            def down(e, n):
                src = w_exp_down[0, bass.ds(e, 1)].rearrange("a (k p) n -> p (a k) n", p=P)
                for k in range(2):
                    sp.dma_start(mraw[n][:, D * k:D * k + D], src[:, k, :]).then_inc(e_landed[n], 16)

            def wait_load_split(ld):
                sp.wait_ge(e_lo, 2 * ld + 2)

            def load_round(r, i, first):
                for k in range(3):
                    l0 = 3 * r - 1 + k
                    if l0 + 12 * first >= MRAW:
                        wait_load_split(l0 - MRAW + 12 * i)
                    elif l0 == 2 * NRAW:
                        sp.wait_ge(out_blocks, 2 * NB)
                    elif l0 == 3 * NRAW:
                        sp.wait_ge(h2_out, 16 * NB)
                        sp.wait_ge(xg_in[1], 16)
                    if l0 + 12 * first >= IN_FLIGHT:
                        sp.wait_ge(e_landed[(l0 - IN_FLIGHT) % MRAW], 32 * ((l0 - IN_FLIGHT) // MRAW + 1) + 32 * i)
                    if k < 2:
                        gate_up(expert(r, i), k, l0 % MRAW)
                    else:
                        down(expert(r, i) - 1, l0 % MRAW)

            sp.wait_ge(lo_done, n_pieces)
            gate_up(0, 0, 0)
            gate_up(0, 1, 1)
            for r in range(1, 5):
                load_round(r, 0, 0)
            with sp.Fori(1, NE // 4 - 1) as i:
                for r in range(1, 5):
                    load_round(r, i, 1)
            for r in range(1, 4):
                load_round(r, NE // 4 - 1, 1)
            wait_load_split(3 * NE - 1 - MRAW)
            down(NE - 1, (3 * NE - 1) % MRAW)

            sp.wait_ge(ov_ready, 1)
            extra = sp.value_load(ovint[0:1, NOV:NOV + 1], min_val=0, max_val=NOV)
            with sp.If(extra > 0):
                sp.wait_ge(e_lo, 6 * NE)
                with sp.Fori(0, NOV) as j:
                    e = sp.value_load(ovint[0:1, bass.ds(j, 1)], min_val=0, max_val=NE - 1)
                    sp.wait_ge(v_id, j + 1)
                    for half in range(2):
                        dst = mraw[half].rearrange("p (k n) -> p k n", n=2 * EH)
                        for m, w in enumerate((w_exp_gate, w_exp_up)):
                            src = w[0, bass.ds(e, 1)].rearrange("a (k p) n -> p (a k) n", p=P)
                            sp.dma_start(dst[:, :, EH * m:EH * m + EH], src[:, 4 * half:4 * half + 4, :]
                                         ).then_inc(v_in, 16)
                    src = w_exp_down[0, bass.ds(e, 1)].rearrange("a (k p) n -> p (a k) n", p=P)
                    sp.dma_start(mraw[2].rearrange("p (k n) -> p k n", n=D), src).then_inc(v_in, 16)
            for i in range(NB):
                sp.wait_ge(fin_ready, i + 1)
                sp.dma_start(out_v[i], h2[:, i, :]).then_inc(out_done, 16)
            sp.wait_ge(out_done, 16 * NB)

        @block.gpsimd
        def _(pool):
            for t in (ident[:, :], zeros[:, :], foxmask, sel_head[:, :, :], sel_row[:, :, :]):
                pool.memset(t, 0.0).then_inc(zeroed, 1)
            pool.memset(valid[:, :], 1.0).then_inc(zeroed, 1)
            pool.wait_ge(zeroed, 6)
            pool.affine_select(out=ident[:, :], in_=ident[:, :], compare_op=ALU.not_equal, fill=1.0, base=0,
                               pattern=[[-1, P]], channel_multiplier=1).then_inc(const_ready, 1)
            for t in (kT[:, :, :], csplit[:, :], nkT[:, :, :], penalty[:, :, :], kcp[:, :, :], vbd[:, :]):
                pool.memset(t, 0.0).then_inc(const_ready, 1)
            for t in range(NE, NE + NOV):
                for half in range(2):
                    pool.dma_start(y_dram[t * P:t * P + P, 512 * half:512 * half + 512], zeros[:, :]
                                   ).then_inc(filled, 16)
            pool.affine_select(out=foxmask, in_=foxmask, compare_op=ALU.is_ge, fill=BIG, base=S - P,
                               pattern=[[-1, S]], channel_multiplier=1).then_inc(const_ready, 1)
            for n in range(3):
                v = sel_head[32 * n:32 * n + 32, :, :]
                pool.wait_ge(const_ready, 8 + n)
                pool.affine_select(out=v, in_=v, compare_op=ALU.not_equal, fill=1.0, base=0,
                                   pattern=[[-1, FOX_H], [0, P]], channel_multiplier=1).then_inc(const_ready, 1)
            pool.wait_ge(const_ready, 11)
            pool.affine_select(out=sel_row[:, :, :], in_=sel_row[:, :, :], compare_op=ALU.not_equal, fill=1.0,
                               base=0, pattern=[[-1, 2], [0, MOBA_BLOCK]], channel_multiplier=1
                               ).then_inc(const_ready, 1)
            pool.affine_select(out=valid[:, :], in_=valid[:, :], compare_op=ALU.is_ge, fill=0.0, base=1 - CMP_LEN,
                               pattern=[[P, NB], [0, NSA_H]], channel_multiplier=1).then_inc(const_ready, 1)
            pool.iota(dist[:, :].bitcast(I32), [[-1, S]], base=S - P, channel_multiplier=1).then_inc(master_ready, 1)
            pool.wait_ge(master_ready, 1)
            pool.tensor_copy(dist[:, :], dist[:, :].bitcast(I32)).then_inc(master_ready, 1)
            pool.wait_ge(master_ready, 2)
            pool.affine_select(out=dist[:, :], in_=dist[:, :], compare_op=ALU.is_ge, fill=BIG * 256, base=S - P,
                               pattern=[[-1, S]], channel_multiplier=1).then_inc(master_ready, 1)
            pool.wait_ge(tp_done, KC + 1)
            pool.iota(cmp_mask.bitcast(I32), [[P, NB], [0, NSA_H], [-CMP_STRIDE, 32]], base=1 - CMP_LEN,
                      channel_multiplier=1).then_inc(master_ready, 1)
            pool.wait_ge(master_ready, 4)
            pool.tensor_copy(cmp_mask, cmp_mask.bitcast(I32)).then_inc(master_ready, 1)
            pool.wait_ge(master_ready, 5)
            for h in range(NSA_H):
                v = cmp_mask.rearrange("p (i h n) -> p i h n", i=NB, h=NSA_H)[:, :, h, :]
                pool.tensor_scalar(v, v, NSA_SLOPES[h], None, ALU.mult).then_inc(master_ready, 1)
            pool.wait_ge(master_ready, N_MASTER0)
            pool.affine_select(out=cmp_mask, in_=cmp_mask, compare_op=ALU.is_ge, fill=BIG,
                               base=1 - CMP_LEN, pattern=[[P, NB], [0, NSA_H], [-CMP_STRIDE, 32]],
                               channel_multiplier=1).then_inc(const_ready, 1)
            made = 0
            for kind, a in seq:
                if kind == "QK" and made < len(master_heads) and a + 1 >= master_from[made]:
                    k, h = master_heads[made]
                    pool.wait_ge(shifted, master_from[made])
                    pool.tensor_scalar(master[:, made % 2, :], dist[:, :], (NSA_SLOPES if k == "s" else MOBA_SLOPES)[h],
                                       None, ALU.mult).then_inc(master_ready, 1)
                    made += 1
                if kind == "T" and pieces[a]["kind"] == "y" and pieces[a]["j"] >= 4:
                    for dd in range(2):
                        g = 2 * pieces[a]["j"] + dd
                        pool.wait_ge(proj_dve, proj_free[(a, dd)][1])
                        pool.tensor_tensor(m_sb[:, g % KC, :], m_sb[:, g % KC, :], shared[:, g % 4, :], ALU.add
                                           ).then_inc(merged, 1)
            pool.wait_ge(m_split, KC)
            pool.memset(ones[:, :], 1.0).then_inc(fconst, 1)
            pool.memset(tri[:, :], 1.0).then_inc(fconst, 1)
            pool.wait_ge(fconst, 2)
            pool.affine_select(out=tri[:, :], in_=tri[:, :], compare_op=ALU.is_gt, fill=0.0, base=0,
                               pattern=[[1, P]], channel_multiplier=-1).then_inc(fconst, 1)

            def indices(dst, width, pattern, base, mult, n):
                pool.iota(iot[:, 0:width], pattern, base=base, channel_multiplier=mult).then_inc(fconst, 1)
                pool.wait_ge(fconst, n + 1)
                pool.tensor_copy(dst, iot[:, 0:width]).then_inc(fconst, 1)
                pool.wait_ge(fconst, n + 2)

            indices(prio[:, :], NB * NE, [[0, NB * NG], [-1, EPG]], EPG, 0, 3)
            indices(eoff[:, :], NE, [[P, NE]], 0, 0, 5)
            indices(tokid[:, 0, :], NB, [[P, NB]], 0, 0, 7)
            indices(tokid[:, 1, :], NB, [[0, NB]], 0, 1, 9)
            indices(jtile[:, :], NOV * NE, [[1, NOV], [0, NE]], 0, 0, 11)
            indices(lane[:, :], P, [[1, P]], 0, 0, 13)
            indices(edge[:, :], NE + NOV + 1, [[P, NE + NOV + 1]], 0, 0, 15)
            pool.wait_ge(g_in, 32)
            for half in range(2):
                for i in range(NB):
                    pool.wait_ge(x1_ready, NB * half + i + 1)
                    cs = slice(512 * half, 512 * half + 512)
                    pool.tensor_tensor(h2[:, i, cs], x1[:, i, cs], gffn[:, cs], ALU.mult).then_inc(gained, 1)
            pool.wait_ge(ids_ready, 1)
            pool.wait_ge(h2_out, 16 * NB)
            for e in range(NE):
                if e >= 2:
                    pool.wait_ge(e_tp, rows_use(e - 2, 0) + 2)
                pool.indirect_dma_start(out=xg[:, e % 2, :], out_offset=None, in_=h2_dram[:, :],
                                        in_offset=bass.IndirectOffsetOnAxis(ap=ids[:, e:e + 1], axis=0)
                                        ).then_inc(xg_in[e % 2], 16)
            pool.wait_ge(filled, 16 * 2 * NOV)
            pool.wait_ge(ov_ready, 1)
            extra = pool.value_load(ovint[0:1, NOV:NOV + 1], min_val=0, max_val=NOV)
            with pool.If(extra > 0):
                pool.wait_ge(e_tp, 3 * NE)
                for j in range(NOV):
                    pool.wait_ge(v_id, j + 1)
                    pool.indirect_dma_start(out=xg[:, 0, :], out_offset=None, in_=h2_dram[:, :],
                                            in_offset=bass.IndirectOffsetOnAxis(ap=ov_id[:, :], axis=0)
                                            ).then_inc(v_gath, 16)
                pool.wait_ge(v_out, 16 * NOV)
            for par in range(2):
                pool.wait_ge(y_out[par], 8 * NE)
            for i in range(NB):
                for c in range(2):
                    pool.indirect_dma_start(out=gathered(i, c), out_offset=None, in_=y_dram[:, :],
                                            in_offset=bass.IndirectOffsetOnAxis(ap=slot_i[:, c, i:i + 1], axis=0)
                                            ).then_inc(back_in[i], 16)

        @block.scalar
        def _(act):
            for i in range(NB):
                act.wait_ge(x_in[i], 16)
                unused = (shared[:, 0:2, :], shared[:, 2:4, :], prob[:, 0:2, :], qT[:, 0:2, :])[i]
                act.activation(unused.rearrange("p a b -> p (a b)"), x_sb[:, i, :], ACT.Square,
                               accum_out=stat[:, 0, i:i + 1]).then_inc(sq_done, 1)
                act.wait_ge(var_ready, i + 1)
                act.activation(stat[:, 2, i:i + 1], stat[:, 1, i:i + 1], ACT.Sqrt).then_inc(std_done, 1)

            def empty_projection(p):
                kind, j = pieces[p]["kind"], pieces[p]["j"]
                use = proj_use[(p, 0)]
                ps = proj_bank[use % 2]
                act.wait_ge(proj_done, use + 1)
                bias = halfb[:, j:j + 1] if kind == "g" else cols[:, p:p + 1]

                def lower(dst, n=S, at=0):
                    return act.activation(dst, ps[0:64, at:at + n], ACT.Identity, bias=bias[0:64])

                def upper(dst, n=S, at=0):
                    return act.activation(dst, ps[64:128, at:at + n], ACT.Identity, bias=bias[64:128])

                def stage_values():
                    n = v_tiles.index(p)
                    if n >= 2:
                        act.wait_ge(tp_done, tp_use[("VT", v_tiles[n - 2])] + 1)
                    act.activation(vstage[:, n % 2, :], ps[:, :], ACT.Identity, bias=bias).then_inc(proj_act, 1)

                if kind in ("fk", "mk"):
                    if kind == "fk":
                        act.wait_ge(const_ready, 2)
                    else:
                        act.wait_ge(o_done, fox_values_used)
                    lower(kT[0:64, 2 * j, :])
                    upper(kT[64:128, 2 * j + 1, :]).then_inc(proj_act, 1)
                elif kind in ("fv", "mv"):
                    stage_values()
                elif kind in ("ss", "sw"):
                    n = 0 if kind == "ss" else 2
                    act.wait_ge(const_ready, 4)
                    lower(nkT[0:64, n, :])
                    lower(nkT[64:128, n + 1, :])
                    stage_values()
                elif kind == "cc":
                    lower(kc2[0:64, :])
                    lower(kc2[64:128, 0:S - 1], S - 1, 1)
                    upper(vc2[0:64, :])
                    upper(vc2[64:128, 0:S - 1], S - 1, 1).then_inc(proj_act, 1)
                else:
                    b, d = divmod(j - 4, KC)
                    if j < 4:
                        wait_emptied(act, o_free, ("CO", NB - 1), o_act, o_dve)
                    elif b == 0:
                        wait_proj_emptied(act, "y", d // 2, d % 2)
                    else:
                        act.wait_ge(merged, KC * (b - 1) + d + 1)
                    act.activation(shared[:, j % 4, :], ps[:, :], ACT.Tanh, bias=bias, scale=0.5
                                   ).then_inc(proj_act, 1)

            for it in seq:
                kind, a = it
                if kind == "COLS":
                    act.wait_ge(tp_done, 1)
                    act.activation(cols[:, :], tp_bank[0][:, 0:R_ALL], ACT.Copy).then_inc(tp_act, 1)
                    act.wait_ge(tp_act, 1)
                    act.activation(halfb[:, :], cols[:, R_GATE:R_NORM], ACT.Copy, scale=0.5).then_inc(bias_halved, 1)
                    act.activation(gcol[:, :], cols[:, R_FFN:R_ALL], ACT.Copy).then_inc(bias_halved, 1)
                    act.wait_ge(bias_halved, 2)
                elif kind == "XT":
                    use = tp_use[it]
                    act.wait_ge(tp_done, use + 1)
                    act.activation(hT_hi[:, a, :], xt_bank(a)[:, :], ACT.Copy,
                                   scale=cols[:, R_NORM + a:R_NORM + a + 1]).then_inc(tp_hi, 1)
                elif kind == "H":
                    ld = ("w", pieces[a]["load"])
                    act.wait_ge(w_landed[slot(ld)], landings[ld])
                    if a >= NSPLIT:
                        wait_piece_used(act, a - NSPLIT)
                    act.activation(piece_split(w_hi, a), piece_raw(a), ACT.Copy).then_inc(hi_done, 1)
                elif kind == "T" and pieces[a]["kind"] not in ("y", "o"):
                    if proj_who((a, 0)) == "act":
                        empty_projection(a)
                elif kind == "SM":
                    act.wait_ge(abs_ready, 1)
                    act.activation(prob[0:FOX_H, 1, :], prob[0:FOX_H, 0, :], ACT.Exp).then_inc(sm_act, 1)
                    act.wait_ge(sm_act, 1)
                    act.activation(prob[0:FOX_H, 2, :], prob[0:FOX_H, 1, :], ACT.Ln, bias=1.0).then_inc(sm_act, 1)
                    wait_tp_emptied(act, it)
                    act.activation(gates[:, :, :], gates[:, :, :], ACT.Exp, scale=-1.0).then_inc(sm_gates, 1)
                elif kind == "QK":
                    act.wait_ge(shifted, a + 1)
                    if a >= NSUM:
                        wait_emptied(act, o_free, ("PV", a - NSUM), o_act, o_dve)
                    pr = prob[:, a % NPROB, 0:unit_width(a)]
                    act.activation(pr, pr, ACT.Exp, bias=negmax[:, a % 4:a % 4 + 1], scale=-1.0,
                                   accum_out=rowsum[:, a % NSUM:a % NSUM + 1]).then_inc(exp_done, 1)
                elif kind == "TR" and tp_who(it) == "act":
                    use, n = tp_use[it], unit_width(a)
                    act.wait_ge(tp_done, use + 1)
                    if a >= NPROBT:
                        act.wait_ge(o_done, o_use[("PV", a - NPROBT)] + 1)
                    act.activation(probT[:, a % NPROBT, 0:n], tp_bank[use % 2][:, 0:n], ACT.Copy).then_inc(tp_act, 1)
                elif kind == "OT":
                    b, pair = a
                    act.wait_ge(tp_done, tp_use[it] + 1)
                    if b == 2:
                        act.wait_ge(proj_done, proj_use[(piece_of[("y", 3)], 1)] + 1)
                    act.activation(oT_hi[:, o_chunk(b, pair), :], tp_bank[tp_use[it] % 2][:, :], ACT.Copy
                                   ).then_inc(tp_hi, 1)
                elif kind in ("CH0", "CH1"):
                    kv, use = int(kind[2]), o_use[it]
                    act.wait_ge(o_done, use + 1)
                    act.wait_ge(tp_done, tp_use[("TR", n_fox - 1)] + 1)
                    act.activation(hidn[:, kv, :], o_bank[use % 2][0:NCMP, 0:CMP_HID], ACT.Gelu_apprx_tanh
                                   ).then_inc(o_act, 1)
                elif kind == "CS":
                    act.wait_ge(c_centered, 1)
                    act.activation(probc, probc, ACT.Exp, scale=-1.0).then_inc(c_exp, 1)
                elif kind == "CT":
                    act.wait_ge(tp_done, tp_use[it] + 1)
                    act.activation(pcT, tp_bank[tp_use[it] % 2][:, :], ACT.Copy).then_inc(tp_act, 1)
                elif kind == "XA":
                    for i in range(NB):
                        act.wait_ge(x1_ready, NB * a + i + 1)
                        act.activation((y_sb if a == 0 else xg)[:, i // 2, 512 * (i % 2):512 * (i % 2) + 512],
                                       x1[:, i, 512 * a:512 * a + 512], ACT.Square,
                                       accum_out=fstat[:, 8 * a, i:i + 1]).then_inc(fsq_done, 1)
                elif kind == "RT" and a % 2 == 0:
                    act.wait_ge(rtp_done, a + 1)
                    if a >= 4:
                        act.wait_ge(logits_mm, a - 3)
                    act.activation(xT[:, a % 4, :], bank[0][:, :], ACT.Copy, scale=gcol[:, a:a + 1]).then_inc(rt_act, 1)
                elif kind == "M":
                    act.wait_ge(proj_done, len(proj_use))
                    for d in range(KC):
                        act.wait_ge(merged, KC + d + 1)
                        act.activation(hT_hi[:, d, :], m_sb[:, d, :], ACT.Copy, scale=0.5).then_inc(m_hi_done, 1)

            act.wait_ge(fvar_ready, 1)
            act.activation(fstat[:, 2, :], fstat[:, 1, :], ACT.Sqrt).then_inc(fstd_done, 1)

            def split_hi(r, i, k):
                m = pc_mod(r, k)
                act.wait_ge(e_landed[m // 2 % MRAW], 32 * (m // (2 * MRAW) + 1) + 32 * i)
                if m >= MSPLIT:
                    act.wait_ge(e_used, pc_no(r, i, k) - MSPLIT + 1)
                act.activation(m_hi[:, m % MSPLIT, :], mraw[m // 2 % MRAW][:, 1024 * (m % 2):1024 * (m % 2) + 1024],
                               ACT.Copy).then_inc(e_hi, 1)

            def rows_hi(r, i):
                for half in range(2):
                    act.wait_ge(e_tp, rows_use(r, i) + half + 1)
                    act.activation(xT_hi[:, r % 2, 4 * half:4 * half + 4, :], four(use_bank(rows_use(r, 0) + half)),
                                   ACT.Copy).then_inc(e_tp_hi, 1)

            def hidden_hi(r, i):
                act.wait_ge(e_tp, hidden_use(r, i) + 1)
                act.activation(hidT_hi[:, r % 2, :, :], two(use_bank(3 * r)), ACT.Copy).then_inc(e_tp_hi, 1)

            def silu(r, i):
                act.wait_ge(e_used, pc_no(r, i, 3) + 1)
                if not_before_2(r, i):
                    act.wait_ge(hid_done, expert(r, i) - 1)
                act.activation(sil[:, r % 2, :], bank[r % 2][:, 0:EH], ACT.Silu).then_inc(sil_done, 1)

            def store_y(r, i):
                act.wait_ge(e_used, 6 * NE if is_last(r, i) else 24 * i + 6 * r + 10)
                if not_before_2(r, i):
                    act.wait_ge(y_out[r % 2], 16 * (2 * i + r // 2))
                for half in range(2):
                    ins = act.activation(y_sb[:, r % 2, 512 * half:512 * half + 512], y_bank(r, half)[:, :], ACT.Copy)
                ins.then_inc(y_done, 1)
                act.wait_ge(y_done, expert(r, i) + 1)
                dst = y_dram.rearrange("(t p) d -> t p d", p=P)[bass.ds(expert(r, i), 1)]
                act.dma_start(dst.rearrange("a p d -> (a p) d"), y_sb[:, r % 2, :]).then_inc(y_out[r % 2], 16)

            def store_rows(i):
                act.wait_ge(gained, NB + i + 1)
                act.wait_ge(root_ready, 1)
                act.activation(h2[:, i, :], h2[:, i, :], ACT.Copy, scale=fstat[:, 3, i:i + 1]).then_inc(h2_ready, 1)
                act.wait_ge(h2_ready, i + 1)
                act.dma_start(h2_dram[i * P:i * P + P, :], h2[:, i, :]).then_inc(h2_out, 16)

            def act_opening():
                split_hi(0, 0, 0)
                split_hi(0, 0, 1)
                act.wait_ge(lg_centered, 1)
                act.activation(rg[:, 2, :], rg[:, 0, :], ACT.Exp)
                act.activation(rt[:, 2, :], rt[:, 1, :], ACT.Exp).then_inc(lg_exp, 1)
                store_rows(0)
                split_hi(0, 0, 2)
                store_rows(1)
                split_hi(0, 0, 3)
                store_rows(2)
                store_rows(3)
                rows_hi(0, 0)
                for k in range(MSPLIT, MSPLIT + 3):
                    split_hi(0, 0, k)
                silu(0, 0)
                rows_hi(1, 0)

            def act_round(r, i):
                split_hi(r, i, 3)
                split_hi(r, i, 4)
                hidden_hi(r - 1, i)
                split_hi(r, i, 5)
                split_hi(r, i, 6)
                silu(r, i)
                if not is_last(r, i):
                    rows_hi(r + 1, i)
                split_hi(r, i, 7)
                if not is_last(r, i):
                    split_hi(r, i, 8)
                store_y(r - 1, i)

            rounds(act, act_opening, act_round)
            hidden_hi(3, NE // 4 - 1)
            store_y(3, NE // 4 - 1)

            act.wait_ge(ov_ready, 1)
            extra = act.value_load(ovint[0:1, NOV:NOV + 1], min_val=0, max_val=NOV)
            with act.If(extra > 0):
                with act.Fori(0, NOV) as j:
                    act.wait_ge(v_gu, j + 1)
                    act.activation(sil[:, 0, :], bank[0][:, 0:EH], ACT.Silu).then_inc(v_sil, 1)
                    act.wait_ge(v_ev, 2 * (j + 1))
                    dst = y_dram.rearrange("(t p) d -> t p d", p=P)[bass.ds(j + NE, 1)]
                    act.dma_start(dst.rearrange("a p d -> (a p) d"), y_sb[:, 0, :]).then_inc(v_out, 16)
            for i in range(NB):
                act.wait_ge(acc_done, 2 * i + 2)
                act.activation(h2[:, i, :], x1[:, i, :], ACT.Square, accum_out=fstat[:, 4, i:i + 1]
                               ).then_inc(nsq_done, 1)
                act.wait_ge(nvar_ready, i + 1)
                act.activation(fstat[:, 6, i:i + 1], fstat[:, 5, i:i + 1], ACT.Sqrt).then_inc(nstd_done, 1)

        @block.vector
        def _(dve):
            steps = [0]

            def link(ins):
                steps[0] += 1
                ins.then_inc(link_dve, 1)
                dve.wait_ge(link_dve, steps[0])

            def inverse_root(var, std, r, t):
                link(dve.reciprocal(r, std))
                link(dve.tensor_tensor(t, var, r, ALU.mult))
                link(dve.tensor_tensor(t, t, r, ALU.mult))
                link(dve.tensor_scalar(t, t, -0.5, 1.5, ALU.mult, ALU.add))
                link(dve.tensor_tensor(r, r, t, ALU.mult))

            dve.memset(rows[:, :], 0.0).then_inc(rows_zero, 1)
            for i in range(NB):
                var, std, root, t = [stat[:, n, i:i + 1] for n in (1, 2, 3, 4)]
                dve.wait_ge(sq_done, i + 1)
                dve.tensor_scalar(var, stat[:, 0, i:i + 1], 1.0 / D, EPS, ALU.mult, ALU.add).then_inc(var_ready, 1)
                dve.wait_ge(var_ready, i + 1)
                dve.wait_ge(std_done, i + 1)
                inverse_root(var, std, root, t)
                dve.tensor_scalar(x_sb[:, i, :], x_sb[:, i, :], root, None, ALU.mult).then_inc(x_scaled, 1)

            def empty_projection(p):
                pc = pieces[p]
                kind, j = pc["kind"], pc["j"]
                if kind == "y":
                    for d in range(2):
                        use, g = proj_use[(p, d)], 2 * j + d
                        dve.wait_ge(proj_done, use + 1)
                        wait_proj_emptied(dve, "g", g)
                        gate = shared[:, g % 4, :]
                        dst = m_sb[:, g % KC, :] if g < KC else gate
                        dve.scalar_tensor_tensor(out=dst, in0=gate, scalar=1.0, in1=proj_bank[use % 2][:, :],
                                                 op0=ALU.add, op1=ALU.mult).then_inc(proj_dve, 1)
                    return
                use = proj_use[(p, 0)]
                ps = proj_bank[use % 2]
                dve.wait_ge(proj_done, use + 1)
                if kind == "sm":
                    n = pc["n"]
                    dve.tensor_scalar(sm_sb, ps[0:n, :], cols[0:n, p:p + 1], None, ALU.add).then_inc(proj_dve, 1)
                    return
                if kind == "mq":
                    dve.wait_ge(o_done, fox_values_used)
                dst = nqT if kind == "nq" else qT
                dve.tensor_scalar(dst[:, j, :], ps[:, :], cols[:, p:p + 1], QSCALE, ALU.add, ALU.mult
                                  ).then_inc(proj_dve, 1)

            def forget_gate(it):
                f = sm_sb[0:FOX_H, :]
                a, t, l = prob[0:FOX_H, 0, :], prob[0:FOX_H, 1, :], prob[0:FOX_H, 2, :]
                link(dve.tensor_scalar(a, f, -1.0, None, ALU.mult))
                dve.tensor_tensor(a, a, f, ALU.min).then_inc(abs_ready, 1)
                dve.wait_ge(tp_done, tp_use[it] + 1)
                n = FOX_H + 3 * NSA_H
                dve.tensor_copy(gates[:, :, :], tp_bank[tp_use[it] % 2][:, 0:NB * n].rearrange(
                    "p (i n) -> p i n", n=n)[:, :, FOX_H:n]).then_inc(tp_dve, 1)
                dve.wait_ge(sm_act, 2)
                link(dve.scalar_tensor_tensor(out=t, in0=f, scalar=0.0, in1=l, op0=ALU.min, op1=ALU.subtract))
                dve.wait_ge(const_ready, 3)
                link(dve.tensor_tensor_scan(a, zeros[0:FOX_H, :], t, 0.0, ALU.add, ALU.add))
                link(dve.tensor_copy(csplit[0:FOX_H, :], a))
                link(dve.tensor_tensor(t, a, csplit[0:FOX_H, :], ALU.subtract))
                link(dve.tensor_copy(cmid[:, :], t))
                link(dve.tensor_tensor(l, t, cmid[:, :], ALU.subtract))
                dve.tensor_copy(csplit[32:32 + FOX_H, :], cmid[:, :])
                dve.tensor_copy(csplit[64:64 + FOX_H, :], l).then_inc(c_ready, 1)
                dve.wait_ge(sm_gates, 1)
                link(dve.tensor_scalar(gates[:, :, :], gates[:, :, :], 1.0, None, ALU.add))
                dve.reciprocal(gates[:, :, :], gates[:, :, :]).then_inc(gates_ready, 1)

            def values_to_tokens(it):
                p, use = it[1], tp_use[it]
                kind, j = pieces[p]["kind"], pieces[p]["j"]
                dve.wait_ge(tp_done, use + 1)
                src = four(tp_bank[use % 2])
                if kind in ("fv", "mv"):
                    if kind == "mv":
                        dve.wait_ge(o_done, fox_values_used)
                    dve.tensor_copy(v_sb[:, :, P * j:P * j + P], src).then_inc(tp_dve, 1)
                else:
                    dve.tensor_copy(nv_sb[:, 0 if kind == "ss" else 1, :, :], src[:, :, 64:128]).then_inc(tp_dve, 1)

            def shift_scores(u):
                kind, h, i = units[u]
                n, use = unit_width(u), sc_use[("QK", u)]
                dve.wait_ge(sc_done, use + 1)
                if kind == "f":
                    dve.wait_ge(const_ready, 8)
                    m = foxmask
                else:
                    mh = master_heads.index(("s" if kind in "sw" else "m", h))
                    dve.wait_ge(master_ready, N_MASTER0 + mh + 1)
                    m = master[:, mh % 2, :]
                if u >= NPROB:
                    dve.wait_ge(tp_done, tp_use[("TR", u - NPROB)] + 1)
                if u >= 4:
                    dve.wait_ge(exp_done, u - 3)
                dve.tensor_tensor_reduce(prob[:, u % NPROB, 0:n], sc_bank[use % 2][:, 0:n], m[:, S - n:S], 1.0, 3e38,
                                         ALU.add, ALU.min, negmax[:, u % 4:u % 4 + 1]).then_inc(shifted, 1)

            def output(u):
                kind, h, i = units[u]
                use, ps = o_use[("PV", u)], None
                ps = o_bank[use % 2][:, 0:HD]
                link(dve.reciprocal(rinv[:, u % 2:u % 2 + 1], rowsum[:, u % NSUM:u % NSUM + 1]))
                if kind in "fm":
                    dve.wait_ge(o_done, use + 1)
                    pair = h // 2 + (0 if kind == "f" else 3)
                    if pair >= 2:
                        b = (0 if pair - 2 < 3 else 2, (pair - 2) % 3)
                        dve.wait_ge(tp_done, tp_use[("OT", b)] + 1)
                    dve.tensor_scalar(obuf[:, pair % 2, i, HD * (h % 2):HD * (h % 2) + HD], ps,
                                      rinv[:, u % 2:u % 2 + 1], None, ALU.mult).then_inc(o_dve, 1)
                else:
                    g = nsa_coef_gate(u)
                    link(dve.tensor_tensor(coef[:, u % 2:u % 2 + 1], rinv[:, u % 2:u % 2 + 1], gates[:, i, g:g + 1],
                                           ALU.mult))
                    dve.wait_ge(o_done, use + 1)
                    if kind == "s":
                        wait_emptied(dve, o_free, ("CO", i), o_act, o_dve)
                    else:
                        wait_emptied(dve, o_free, ("PV", u - NB), o_act, o_dve)
                    dst = onsa[:, i, HD * h:HD * h + HD]
                    dve.scalar_tensor_tensor(out=dst, in0=ps, scalar=coef[:, u % 2:u % 2 + 1], in1=dst, op0=ALU.mult,
                                             op1=ALU.add).then_inc(o_dve, 1)

            for it in seq:
                kind, a = it
                if kind == "XT":
                    use = tp_use[it]
                    dve.wait_ge(tp_hi, a + 1)
                    dve.scalar_tensor_tensor(out=hT_lo[:, a, :], in0=xt_bank(a)[:, :],
                                             scalar=cols[:, R_NORM + a:R_NORM + a + 1],
                                             in1=hT_hi[:, a, :].bitcast(F32), op0=ALU.mult, op1=ALU.subtract
                                             ).then_inc(tp_dve, 1)
                elif kind == "H":
                    dve.wait_ge(hi_done, a + 1)
                    dve.tensor_tensor(piece_split(w_lo, a), piece_raw(a), piece_split(w_hi, a).bitcast(F32),
                                      ALU.subtract).then_inc(lo_done, 1)
                elif kind == "T" and pieces[a]["kind"] != "o":
                    if proj_who((a, 0)) == "dve":
                        empty_projection(a)
                    if pieces[a]["kind"] == "sm":
                        wait_proj_emptied(dve, "sm", 0)
                elif kind == "SM":
                    forget_gate(it)
                elif kind == "VT":
                    values_to_tokens(it)
                elif kind == "KS":
                    wait_proj_emptied(dve, "mk", a)
                    for h in range(2):
                        ins = dve.tensor_reduce(ksum[:, a, h:h + 1], kT[:, 2 * a + h, 0:MOBA_BLOCK], AX_X, ALU.add)
                    ins.then_inc(ksum_ready, 1)
                    dve.wait_ge(o_done, o_use[it] + 1)
                    dve.wait_ge(const_ready, 5)
                    dve.tensor_scalar(penalty[0:2, a, :], o_bank[o_use[it] % 2][0:2, 0:MOBA_BLOCK],
                                      QSCALE * MOBA_BLOCK * INVALID_SCORE, BIG, ALU.is_gt, ALU.mult).then_inc(o_dve, 1)
                elif kind == "QK":
                    shift_scores(a)
                elif kind == "TR" and tp_who(it) == "dve":
                    use, n = tp_use[it], unit_width(a)
                    dve.wait_ge(tp_done, use + 1)
                    if a >= NPROBT:
                        dve.wait_ge(o_done, o_use[("PV", a - NPROBT)] + 1)
                    dve.tensor_copy(probT[:, a % NPROBT, 0:n], tp_bank[use % 2][:, 0:n]).then_inc(tp_dve, 1)
                elif kind == "PV":
                    output(a)
                elif kind == "OT":
                    b, pair = a
                    dve.wait_ge(tp_hi, KC + 1 + [o[1] for o in seq if o[0] == "OT"].index(a))
                    dve.tensor_tensor(oT_lo[:, o_chunk(b, pair), :], tp_bank[tp_use[it] % 2][:, :],
                                      oT_hi[:, o_chunk(b, pair), :].bitcast(F32), ALU.subtract).then_inc(tp_dve, 1)
                elif kind == "CB":
                    wait_proj_emptied(dve, "cc", 0)
                    for kv, src in enumerate((kc2, vc2)):
                        turned = src.rearrange("p (n r) -> p r n", r=CMP_STRIDE)[:, 0:CMP_STRIDE:2, :]
                        for half in range(2):
                            c0 = R_POS + 16 * kv + 8 * half
                            pos = cols[:, c0:c0 + 8].unsqueeze(2).broadcast_to([P, 8, NCMP])
                            ins = dve.tensor_tensor(cblk[:, 16 * kv + 8 * half:16 * kv + 8 * half + 8, 0:NCMP],
                                                    turned[:, :, half:half + NCMP], pos, ALU.add)
                    ins.then_inc(cblk_ready, 1)
                elif kind == "CX":
                    dve.wait_ge(tp_done, tp_use[it] + 1)
                    dve.tensor_copy(hidc[:, :, 0:NCMP], tp_bank[tp_use[it] % 2][:, 0:P].rearrange(
                        "p (n c) -> p n c", n=4)[:, :, 0:NCMP]).then_inc(tp_dve, 1)
                elif kind == "CK":
                    use = o_use[it]
                    ps = o_bank[use % 2]
                    dve.wait_ge(o_done, use + 1)
                    dve.wait_ge(const_ready, 7)
                    dve.tensor_copy(kcp[0:64, 0, 0:NCMP], ps[0:64, 0:NCMP])
                    dve.tensor_copy(kcp[64:128, 1, 0:NCMP], ps[0:64, 0:NCMP])
                    for h in range(NSA_H):
                        ins = dve.tensor_copy(vbd[32 * h:32 * h + NCMP, HD * h:HD * h + HD], ps[0:NCMP, 64:64 + HD])
                    ins.then_inc(o_dve, 1)
                elif kind == "CS":
                    groups = probc.rearrange("p (g n) -> p g n", n=32)
                    mn, sm, rs, co = [cstat[:, n, :] for n in range(4)]
                    dve.wait_ge(sc_done, sc_use[it] + 1)
                    dve.wait_ge(const_ready, 14)
                    dve.tensor_tensor(probc, sc_bank[sc_use[it] % 2][:, :], cmp_mask, ALU.add).then_inc(c_shifted, 1)
                    dve.wait_ge(c_shifted, 1)
                    link(dve.tensor_reduce(mn, groups, AX_X, ALU.min))
                    dve.tensor_tensor(groups, groups, mn.unsqueeze(2).broadcast_to([P, 16, 32]), ALU.subtract
                                      ).then_inc(c_centered, 1)
                    dve.wait_ge(c_exp, 1)
                    link(dve.tensor_reduce(sm, groups, AX_X, ALU.add))
                    link(dve.reciprocal(rs, sm))
                    link(dve.tensor_tensor(rs, rs, valid[:, :], ALU.mult))
                    dve.wait_ge(gates_ready, 1)
                    link(dve.tensor_tensor(co.rearrange("p (i h) -> p i h", i=NB),
                                           rs.rearrange("p (i h) -> p i h", i=NB), gates[:, :, 0:NSA_H], ALU.mult))
                elif kind == "CO":
                    for i in range(NB):
                        use = o_use[("CO", i)]
                        dve.wait_ge(o_done, use + 1)
                        co = cstat[:, 3, NSA_H * i:NSA_H * i + NSA_H].unsqueeze(2).broadcast_to([P, NSA_H, HD])
                        dve.tensor_tensor(onsa[:, i, :].rearrange("p (h d) -> p h d", h=NSA_H),
                                          o_bank[use % 2][:, 0:NSA_H * HD].rearrange("p (h d) -> p h d", h=NSA_H),
                                          co, ALU.mult).then_inc(o_dve, 1)
                elif kind == "XA":
                    if a == 0:
                        dve.wait_ge(x_again, 16 * NB)
                    for i in range(NB):
                        dve.wait_ge(out_blocks, NB * a + i + 1)
                        part = x1[:, i, 512 * a:512 * a + 512]
                        dve.tensor_tensor(part, part, bank[4 * a + i][:, :], ALU.add).then_inc(x1_ready, 1)
                elif kind == "RT" and a % 2 == 1:
                    dve.wait_ge(rtp_done, a + 1)
                    if a >= 4:
                        dve.wait_ge(logits_mm, a - 3)
                    dve.tensor_scalar(xT[:, a % 4, :], bank[1][:, :], gcol[:, a:a + 1], None, ALU.mult
                                      ).then_inc(rt_dve, 1)
                elif kind == "M":
                    for d in range(KC):
                        dve.wait_ge(m_hi_done, d + 1)
                        dve.scalar_tensor_tensor(out=hT_lo[:, d, :], in0=m_sb[:, d, :], scalar=0.5,
                                                 in1=hT_hi[:, d, :].bitcast(F32), op0=ALU.mult, op1=ALU.subtract
                                                 ).then_inc(m_split, 1)

            def split_lo(r, i, k):
                m = pc_mod(r, k)
                dve.wait_ge(e_hi, pc_no(r, i, k) + 1)
                dve.tensor_tensor(m_lo[:, m % MSPLIT, :], mraw[m // 2 % MRAW][:, 1024 * (m % 2):1024 * (m % 2) + 1024],
                                  m_hi[:, m % MSPLIT, :].bitcast(F32), ALU.subtract).then_inc(e_lo, 1)

            dve.wait_ge(fsq_done, 2 * NB)
            link(dve.tensor_tensor(fstat[:, 1, :], fstat[:, 0, :], fstat[:, 8, :], ALU.add))
            dve.tensor_scalar(fstat[:, 1, :], fstat[:, 1, :], 1.0 / D, EPS, ALU.mult, ALU.add).then_inc(fvar_ready, 1)
            dve.wait_ge(logits_mm, KC)
            dve.tensor_copy(lgT[:, :], bank[2][0:NG + NE, :]).then_inc(lgT_ready, 1)
            dve.wait_ge(fvar_ready, 1)
            dve.wait_ge(fstd_done, 1)
            inverse_root(fstat[:, 1, :], fstat[:, 2, :], fstat[:, 3, :], fstat[:, 7, :])
            root = fstat[:, 3, :]

            tok_g = [P, NB, NG]
            tok_ge = [P, NB * NG, EPG]
            tok_e = [P, NB, NE]

            def each_group(v):
                return v.rearrange("p (i g) -> p i g", i=NB)

            def in_groups(v):
                return v.rearrange("p (q e) -> p q e", e=EPG)

            def by_expert(v):
                return v.rearrange("p (i e) -> p i e", i=NB)

            G, E = lg[:, :, 0:NG], lg[:, :, NG:NG + NE]
            dve.wait_ge(lgT_done, 1)
            tok_l = [P, NB, NG + NE]
            dve.tensor_tensor(lg[:, :, :], bank[3][:, 0:NB * (NG + NE)].rearrange("p (i n) -> p i n", i=NB),
                              root.unsqueeze(2).broadcast_to(tok_l), ALU.mult).then_inc(root_ready, 1)
            dve.wait_ge(root_ready, 1)
            link(dve.tensor_tensor(lg[:, :, :], lg[:, :, :], b_rt[:, :].unsqueeze(1).broadcast_to(tok_l), ALU.add))
            gmax, gsum, gkey, m2sum, wden, winv, w_a, w_b = [rw[:, n, :] for n in range(8)]
            slot_a, slot_b = rw[:, 8, :], rw[:, 9, :]
            gc, emax, gexp, gkeys, gsel, ekmax, m2, ekmax2 = [rg[:, n, :] for n in range(8)]
            ec, eexp, ekeys, sel_a, rest, ekeys2, sel_b, sel, pos, slots = [rt[:, n, :] for n in range(1, 11)]
            link(dve.tensor_reduce(gmax, G, AX_X, ALU.max))
            link(dve.tensor_tensor(each_group(gc), G, gmax.unsqueeze(2).broadcast_to(tok_g), ALU.subtract))
            link(dve.tensor_copy(by_expert(rt[:, 0, :]), E))
            link(dve.tensor_reduce(emax, in_groups(rt[:, 0, :]), AX_X, ALU.max))
            dve.tensor_tensor(in_groups(ec), in_groups(rt[:, 0, :]), emax.unsqueeze(2).broadcast_to(tok_ge),
                              ALU.subtract).then_inc(lg_centered, 1)
            dve.wait_ge(lg_centered, 1)
            dve.wait_ge(fconst, 17)
            link(dve.scalar_tensor_tensor(out=gkeys, in0=gc, scalar=0.0, in1=prio[:, 0:NB * NG], op0=ALU.is_ge,
                                          op1=ALU.mult))
            link(dve.tensor_reduce(gkey, each_group(gkeys), AX_X, ALU.max))
            link(dve.tensor_tensor(each_group(gsel), each_group(gkeys), gkey.unsqueeze(2).broadcast_to(tok_g),
                                   ALU.is_equal))
            link(dve.scalar_tensor_tensor(out=ekeys, in0=ec, scalar=0.0, in1=prio[:, :], op0=ALU.is_ge, op1=ALU.mult))
            link(dve.tensor_reduce(ekmax, in_groups(ekeys), AX_X, ALU.max))
            link(dve.tensor_tensor(in_groups(sel_a), in_groups(ekeys), ekmax.unsqueeze(2).broadcast_to(tok_ge),
                                   ALU.is_equal))
            dve.wait_ge(lg_exp, 1)
            link(dve.scalar_tensor_tensor(out=rest, in0=sel_a, scalar=-2.0, in1=eexp, op0=ALU.mult, op1=ALU.add))
            link(dve.tensor_reduce(m2, in_groups(rest), AX_X, ALU.max))
            link(dve.tensor_tensor(in_groups(ekeys2), in_groups(rest), m2.unsqueeze(2).broadcast_to(tok_ge),
                                   ALU.is_equal))
            link(dve.tensor_tensor(ekeys2, ekeys2, prio[:, :], ALU.mult))
            link(dve.tensor_reduce(ekmax2, in_groups(ekeys2), AX_X, ALU.max))
            link(dve.tensor_tensor(in_groups(sel_b), in_groups(ekeys2), ekmax2.unsqueeze(2).broadcast_to(tok_ge),
                                   ALU.is_equal))
            link(dve.tensor_tensor(in_groups(sel_a), in_groups(sel_a), gsel.unsqueeze(2).broadcast_to(tok_ge),
                                   ALU.mult))
            link(dve.tensor_tensor(in_groups(sel_b), in_groups(sel_b), gsel.unsqueeze(2).broadcast_to(tok_ge),
                                   ALU.mult))
            dve.tensor_tensor(selb[:, :], sel_a, sel_b, ALU.add).then_inc(sel_ready, 1)
            cnt, over, upto, base = [ecnt[:, n, :] for n in range(4)]
            dve.wait_ge(pos_mm, 1)
            link(dve.tensor_copy(pos, bank[1][:, 0:NB * NE]))
            link(dve.tensor_copy(cnt, bank[1][:, NB * NE:NB * NE + NE]))
            link(dve.tensor_scalar(over, cnt, float(P), None, ALU.is_gt))
            for n in (2, 3):
                link(dve.scalar_tensor_tensor(out=over, in0=cnt, scalar=float(n * P), in1=over, op0=ALU.is_gt,
                                              op1=ALU.add))
            link(dve.tensor_tensor_scan(upto, zeros[:, 0:NE], over, 0.0, ALU.add, ALU.add))
            link(dve.tensor_tensor(base, upto, over, ALU.subtract))
            link(dve.tensor_scalar(base, base, float(P), float(NE * P - P), ALU.mult, ALU.add))
            link(dve.tensor_tensor(base, base, eoff[:, :], ALU.subtract))
            link(dve.scalar_tensor_tensor(out=by_expert(slots), in0=by_expert(pos), scalar=float(P),
                                          in1=base.unsqueeze(1).broadcast_to(tok_e), op0=ALU.is_ge, op1=ALU.mult))
            link(dve.tensor_tensor(slots, slots, pos, ALU.add))
            link(dve.tensor_tensor(by_expert(slots), by_expert(slots), eoff[:, :].unsqueeze(1).broadcast_to(tok_e),
                                   ALU.add))
            for c, (s_, dst) in enumerate(((sel_a, slot_a), (sel_b, slot_b))):
                link(dve.tensor_tensor(pos, s_, slots, ALU.mult))
                link(dve.tensor_reduce(dst, by_expert(pos), AX_X, ALU.add))
                link(dve.tensor_copy(slot_i[:, c, :], dst))
            slots_ab, tile_ab, lane_ab = rw[:, 8:10, :].rearrange("p c i -> p (c i)"), tiles[:, 0, :], tiles[:, 1, :]
            nt = NE + NOV
            link(dve.tensor_tensor(atleast[:, :, :], slots_ab.unsqueeze(2).broadcast_to([P, 2 * NB, nt + 1]),
                                   edge[:, :].unsqueeze(1).broadcast_to([P, 2 * NB, nt + 1]), ALU.is_ge))
            link(dve.tensor_reduce(tile_ab, atleast[:, :, :], AX_X, ALU.add))
            link(dve.scalar_tensor_tensor(out=lane_ab, in0=tile_ab, scalar=-float(P), in1=slots_ab, op0=ALU.mult,
                                          op1=ALU.add))
            link(dve.tensor_scalar(lane_ab, lane_ab, float(P), None, ALU.add))
            dve.tensor_tensor(in_lane, lane_ab.unsqueeze(2).broadcast_to([P, 2 * NB, P]),
                              lane[:, :].unsqueeze(1).broadcast_to([P, 2 * NB, P]), ALU.is_equal
                              ).then_inc(onehot_ready, 1)
            link(dve.tensor_tensor(in_tile[:, :, :], atleast[:, :, 0:nt], atleast[:, :, 1:nt + 1], ALU.subtract))
            for part in range(2):
                for c in range(2):
                    dve.tensor_tensor(part_id[:, part, NB * c:NB * c + NB, :], in_tile[:, NB * c:NB * c + NB, :],
                                      tokid[:, part, :].unsqueeze(2).broadcast_to([P, NB, nt]), ALU.mult
                                      ).then_inc(onehot_ready, 1)
            dve.wait_ge(ids_mm, 1)
            dve.tensor_copy(ids[:, :], bank[3][:, 0:nt]).then_inc(ids_ready, 1)
            for k in range(MSPLIT):
                split_lo(0, 0, k)
            link(dve.tensor_reduce(gsum, each_group(gexp), AX_X, ALU.add))
            link(dve.tensor_tensor(gkeys, gsel, m2, ALU.mult))
            link(dve.tensor_reduce(m2sum, each_group(gkeys), AX_X, ALU.add))
            link(dve.scalar_tensor_tensor(out=wden, in0=m2sum, scalar=1.0, in1=gsum, op0=ALU.add, op1=ALU.mult))
            link(dve.reciprocal(w_a, wden))
            link(dve.tensor_tensor(w_b, w_a, m2sum, ALU.mult))
            link(dve.tensor_tensor(ovmap[:, :].rearrange("p (j e) -> p j e", j=NOV),
                                   upto.unsqueeze(1).broadcast_to([P, NOV, NE]),
                                   jtile[:, :].rearrange("p (j e) -> p j e", j=NOV), ALU.is_le))
            link(dve.tensor_reduce(ovcnt[:, 0:NOV], ovmap[:, :].rearrange("p (j e) -> p j e", j=NOV), AX_X, ALU.add))
            link(dve.tensor_scalar(ovcnt[:, 0:NOV], ovcnt[:, 0:NOV], float(NE - 1), None, ALU.min))
            link(dve.tensor_copy(ovcnt[:, NOV:NOV + 1], upto[:, NE - 1:NE]))
            dve.tensor_copy(ovint[:, :], ovcnt[:, :]).then_inc(ov_ready, 1)

            def rows_lo(r, i):
                for half in range(2):
                    dve.wait_ge(e_tp_hi, rows_use(r, i) + half + 1)
                    dst = (r % 2, slice(4 * half, 4 * half + 4))
                    dve.tensor_tensor(xT_lo[:, dst[0], dst[1], :], four(use_bank(rows_use(r, 0) + half)),
                                      xT_hi[:, dst[0], dst[1], :].bitcast(F32), ALU.subtract).then_inc(e_tp_free, 1)

            def hidden_lo(r, i):
                dve.wait_ge(e_tp_hi, hidden_use(r, i) + 1)
                dve.tensor_tensor(hidT_lo[:, r % 2, :, :], two(use_bank(3 * r)),
                                  hidT_hi[:, r % 2, :, :].bitcast(F32), ALU.subtract).then_inc(e_tp_free, 1)

            def hidden(r, i):
                dve.wait_ge(sil_done, expert(r, i) + 1)
                if not_before_2(r, i):
                    dve.wait_ge(e_tp, hidden_use(r - 2, i) + 1)
                dve.tensor_tensor(hid[:, r % 2, :], sil[:, r % 2, :], bank[r % 2][:, EH:2 * EH], ALU.mult
                                  ).then_inc(hid_done, 1)

            def dve_opening():
                rows_lo(0, 0)
                for k in range(MSPLIT, MSPLIT + 3):
                    split_lo(0, 0, k)
                hidden(0, 0)
                rows_lo(1, 0)

            def dve_round(r, i):
                split_lo(r, i, 3)
                split_lo(r, i, 4)
                hidden_lo(r - 1, i)
                split_lo(r, i, 5)
                split_lo(r, i, 6)
                hidden(r, i)
                if not is_last(r, i):
                    rows_lo(r + 1, i)
                split_lo(r, i, 7)
                if not is_last(r, i):
                    split_lo(r, i, 8)

            rounds(dve, dve_opening, dve_round)
            hidden_lo(3, NE // 4 - 1)

            dve.wait_ge(ov_ready, 1)
            extra = dve.value_load(ovint[0:1, NOV:NOV + 1], min_val=0, max_val=NOV)
            with dve.If(extra > 0):
                for par in range(2):
                    dve.wait_ge(y_out[par], 8 * NE)
                with dve.Fori(0, NOV) as j:
                    dve.tensor_copy(ov_id[:, :], ids[:, bass.ds(j + NE, 1)]).then_inc(v_id, 1)
                    for half in range(2):
                        dve.wait_ge(v_tp, 2 * j + half + 1)
                        dve.tensor_copy(h2T[:, 0, 512 * half:512 * half + 512], tp_bank[half][:, :]).then_inc(v_xT, 1)
                    dve.wait_ge(v_sil, j + 1)
                    dve.tensor_tensor(hid[:, 0, :], sil[:, 0, :], bank[0][:, EH:2 * EH], ALU.mult).then_inc(v_hid, 1)
                    dve.wait_ge(v_htp, j + 1)
                    dve.tensor_copy(h2T[:, 1, 0:2 * P], tp_bank[0][:, 0:2 * P]).then_inc(v_hT, 1)
                    for half in range(2):
                        dve.wait_ge(v_y, 2 * j + half + 1)
                        dve.tensor_copy(y_sb[:, 0, 512 * half:512 * half + 512], bank[2 + half][:, :]).then_inc(v_ev, 1)
                    dve.wait_ge(v_out, 16 * (j + 1))
            def add_results(i):
                dve.wait_ge(back_in[i], 32)
                for c, w in enumerate((w_a, w_b)):
                    dve.scalar_tensor_tensor(out=x1[:, i, :], in0=gathered(i, c), scalar=w[:, i:i + 1],
                                             in1=x1[:, i, :], op0=ALU.mult, op1=ALU.add).then_inc(acc_done, 1)
                    dve.wait_ge(acc_done, 2 * i + c + 1)

            def last_norm(i):
                var, std, t = [fstat[:, n, i:i + 1] for n in (5, 6, 7)]
                dve.wait_ge(nsq_done, i + 1)
                dve.tensor_scalar(var, fstat[:, 4, i:i + 1], 1.0 / D, EPS, ALU.mult, ALU.add).then_inc(nvar_ready, 1)
                dve.wait_ge(nvar_ready, i + 1)
                dve.wait_ge(nstd_done, i + 1)
                inverse_root(var, std, fstat[:, 3, i:i + 1], t)
                dve.scalar_tensor_tensor(out=h2[:, i, :], in0=x1[:, i, :], scalar=fstat[:, 3, i:i + 1], in1=gfin[:, :],
                                         op0=ALU.mult, op1=ALU.mult).then_inc(fin_ready, 1)

            add_results(0)
            for i in range(1, NB):
                add_results(i)
                last_norm(i - 1)
            last_norm(NB - 1)

        @block.tensor
        def _(pe):
            def three(out_, a_hi, a_lo, b_hi, b_lo, start, stop):
                pe.matmul(out_, a_hi, b_hi, start=start, stop=False)
                pe.matmul(out_, a_hi, b_lo, start=False, stop=False)
                return pe.matmul(out_, a_lo, b_hi, start=False, stop=stop)

            def take(uses, order_, key, counts, act_sem, dve_sem):
                n = uses[key]
                if n >= 2:
                    wait_emptied(pe, counts, order_[n - 2], act_sem, dve_sem)
                return n % 2

            def take_tp(it):
                return tp_bank[take(tp_use, at_tp, it, tp_free, tp_act, tp_dve)]

            def take_o(key):
                return o_bank[take(o_use, at_o, key, o_free, o_act, o_dve)]

            def take_proj(key):
                return proj_bank[take(proj_use, at_proj, key, proj_free, proj_act, proj_dve)]

            def take_sc(it):
                n = sc_use[it]
                if n >= 2:
                    was = at_sc[n - 2]
                    if was[0] == "CS":
                        pe.wait_ge(c_shifted, 1)
                    else:
                        pe.wait_ge(shifted, was[1] + 1)
                return sc_bank[n % 2]

            def project(p):
                pc = pieces[p]
                pe.wait_ge(lo_done, p + 1)
                wh, wl = piece_split(w_hi, p), piece_split(w_lo, p)
                if pc["kind"] == "o":
                    half, k0 = pc["j"] // 4, 2 * (pc["j"] % 4)
                    last = k0 == KC - 2
                    for kk, i in [(kk, i) for i in range(NB) for kk in range(2)] if last else [
                            (kk, i) for kk in range(2) for i in range(NB)]:
                        k, t = k0 + kk, slice(P * i, P * i + P)
                        if half == 0:
                            pe.wait_ge(m_split, k + 1)
                        ins = three(bank[4 * half + i][:, :], hT_hi[:, k, t], hT_lo[:, k, t], wh[:, kk, :],
                                    wl[:, kk, :], k == 0, k == KC - 1)
                        if k == KC - 1:
                            ins.then_inc(out_blocks, 1)
                    if not last:
                        ins.then_inc(out_mm, 1)
                    return
                for d in range(2 if pc["kind"] == "y" else 1):
                    ps = take_proj((p, d))
                    for k in range(pc["k"]):
                        if pc["kind"] == "y":
                            b = pc["j"] // 4
                            if k == 0 and d == 0:
                                for pair in range(pc["k"]):
                                    wait_tp_emptied(pe, ("OT", (b, pair)))
                            c = o_chunk(b, k)
                            rh, rl, cols_ = oT_hi[:, c, :], oT_lo[:, c, :], slice(P * d, P * d + P)
                        else:
                            if p == 0:
                                wait_tp_emptied(pe, ("XT", k))
                            rh, rl, cols_ = hT_hi[:, k, :], hT_lo[:, k, :], slice(0, pc["n"])
                        n = P if pc["kind"] == "y" else pc["n"]
                        ins = three(ps[0:n, :], wh[:, k, cols_], wl[:, k, cols_], rh, rl, k == 0, k == pc["k"] - 1)
                    ins.then_inc(proj_done, 1)

            def scores(u):
                kind, h, i = units[u]
                if u == 0:
                    for key in (("fq", 2), ("fk", 2)):
                        wait_proj_emptied(pe, *key)
                    pe.wait_ge(c_ready, 1)
                    pe.wait_ge(const_ready, 11)
                if u == n_fox:
                    for key in (("nq", 1), ("ss", 0), ("sw", 0)):
                        wait_proj_emptied(pe, *key)
                if u == n_fox + 2 * NSA_H * NB:
                    for key in (("mq", 2), ("mk", 2)):
                        wait_proj_emptied(pe, *key)
                    wait_emptied(pe, o_free, ("KS", 2), o_act, o_dve)
                    pe.wait_ge(const_ready, 12)
                n = unit_width(u)
                ps = take_sc(("QK", u))
                q = (qT if kind in "fm" else nqT)[:, h // 2, P * i:P * i + P]
                k = kT[:, h, 0:n] if kind in "fm" else nkT[:, (0 if kind == "s" else 2) + h % 2, 0:n]
                extra_ = kind == "f" or (kind == "m" and i >= 2)
                ins = pe.matmul(ps[:, 0:n], q, k, start=True, stop=kind != "f")
                if kind == "f":
                    ins = pe.matmul(ps[:, 0:n], sel_head[:, h, :], csplit[:, 0:n], start=False, stop=True)
                elif extra_:
                    ins = pe.matmul(ps[:, 0:MOBA_BLOCK], penalty[:, h // 2, P * (i - 2):P * (i - 1)],
                                    sel_row[:, h % 2, :], start=False, stop=True, skip_group_check=True)
                ins.then_inc(sc_done, 1)

            def transposed(u):
                it = ("TR", u)
                pe.wait_ge(exp_done, u + 1)
                ps = take_tp(it)
                for c in range(units[u][2] + 1):
                    ins = pe.transpose(ps[:, P * c:P * c + P], prob[:, u % NPROB, P * c:P * c + P], ident[:, :])
                ins.then_inc(tp_done, 1)

            def values(u):
                kind, h, i = units[u]
                if i == 0:
                    tile = {"f": "fv", "m": "mv", "s": "ss", "w": "sw"}[kind]
                    wait_tp_emptied(pe, ("VT", piece_of[(tile, h // 2 if kind in "fm" else 0)]))
                wait_tp_emptied(pe, ("TR", u))
                ps = take_o(("PV", u))
                for c in range(i + 1):
                    v = v_sb[:, c, HD * h:HD * h + HD] if kind in "fm" else nv_sb[:, 0 if kind == "s" else 1, c, :]
                    ins = pe.matmul(ps[:, 0:HD], probT[:, u % NPROBT, P * c:P * c + P], v, start=(c == 0), stop=(c == i))
                ins.then_inc(o_done, 1)

            def router_product(k):
                if k % 2 == 0:
                    pe.wait_ge(rt_act, k // 2 + 1)
                else:
                    pe.wait_ge(rt_dve, k // 2 + 1)
                pe.matmul(bank[2][0:NG + NE, :], w_rt[:, k, :], xT[:, k % 4, :], start=(k == 0), stop=(k == KC - 1)
                          ).then_inc(logits_mm, 1)

            pe.wait_ge(rows_in, 16 * 9)
            pe.wait_ge(const_ready, 1)
            for it in seq:
                kind, a = it
                if kind == "COLS":
                    pe.transpose(take_tp(it)[:, 0:R_ALL], rows[0:R_ALL, :], ident[0:R_ALL, 0:R_ALL]).then_inc(tp_done, 1)
                elif kind == "XT":
                    if a == 0:
                        pe.wait_ge(x_scaled, NB)
                    if a >= 5:
                        wait_tp_emptied(pe, ("XT", a - 6) if a > 5 else ("COLS", 0))
                    ps = xt_bank(a)
                    for i in range(NB):
                        ins = pe.transpose(ps[:, P * i:P * i + P], x_sb[:, i, P * a:P * a + P], ident[:, :])
                    ins.then_inc(tp_done, 1)
                elif kind == "T":
                    project(a)
                elif kind == "VT":
                    wait_emptied(pe, proj_free, (a, 0), proj_act, proj_dve)
                    ps = take_tp(it)
                    for i in range(NB):
                        ins = pe.transpose(ps[:, P * i:P * i + P], vstage[:, v_tiles.index(a) % 2, P * i:P * i + P],
                                           ident[:, :])
                    ins.then_inc(tp_done, 1)
                elif kind == "SM":
                    wait_proj_emptied(pe, "sm", 0)
                    n = FOX_H + 3 * NSA_H
                    ps = take_tp(it)
                    for i in range(NB):
                        ins = pe.transpose(ps[:, n * i:n * i + n], sm_sb[:, P * i:P * i + P], ident[0:n, 0:n])
                    ins.then_inc(tp_done, 1)
                elif kind == "KS":
                    pe.wait_ge(ksum_ready, a + 1)
                    wait_proj_emptied(pe, "mq", a)
                    pe.matmul(take_o(it)[0:2, 0:MOBA_BLOCK], ksum[:, a, :], qT[:, a, MOBA_BLOCK:S], start=True,
                              stop=True).then_inc(o_done, 1)
                elif kind == "QK":
                    scores(a)
                elif kind == "TR":
                    transposed(a)
                elif kind == "PV":
                    values(a)
                elif kind == "OT":
                    b, pair = a
                    last = max(u for u, (k_, h_, _) in enumerate(units) if k_ == "fwm"[b] and h_ // 2 == pair)
                    wait_emptied(pe, o_free, ("PV", last), o_act, o_dve)
                    ps = take_tp(it)
                    for i in range(NB):
                        src = (onsa[:, i, P * pair:P * pair + P] if b == 1
                               else obuf[:, (pair + (3 if b == 2 else 0)) % 2, i, :])
                        ins = pe.transpose(ps[:, P * i:P * i + P], src, ident[:, :])
                    ins.then_inc(tp_done, 1)
                elif kind in ("CH0", "CH1"):
                    kv = int(kind[2])
                    pe.wait_ge(cblk_ready, 1)
                    ps = take_o(it)
                    for cw in range(2):
                        ld = ("c", 2 * kv + cw)
                        pe.wait_ge(w_landed[slot(ld)], landings[ld])
                    for c in range(16):
                        ins = pe.matmul(ps[0:NCMP, 0:CMP_HID], cblk[:, 16 * kv + c, 0:NCMP],
                                        slot_tile(("c", 2 * kv + c // 8), CMP_HID)[:, c % 8, :],
                                        start=(c == 0), stop=(c == 15))
                        if c == 7:
                            ins.then_inc(cw_used, 1)
                    for hh in range(2):
                        row = R_B1 + 2 * kv + hh
                        ins = pe.matmul(ps[0:NCMP, P * hh:P * hh + P],
                                        ident[0:R_ALL, row:row + 1].broadcast_to([R_ALL, NCMP]), rows[0:R_ALL, :],
                                        start=False, stop=True, skip_group_check=True)
                    ins.then_inc(o_done, 1)
                elif kind == "RT":
                    pe.wait_ge(x1_ready, NB * (a // 4) + NB)
                    if a >= 2:
                        pe.wait_ge(rt_act if a % 2 == 0 else rt_dve, a // 2)
                    for i in range(NB):
                        ins = pe.transpose(bank[a % 2][:, P * i:P * i + P], x1[:, i, P * a:P * a + P], ident[:, :])
                    ins.then_inc(rtp_done, 1)
                    if a % 4 > 0:
                        router_product(a - 1)
                    if a % 4 == 3:
                        router_product(a)
                elif kind == "CX":
                    wait_emptied(pe, o_free, ("CH1", 0), o_act, o_dve)
                    ps = take_tp(it)
                    for n in range(4):
                        ins = pe.transpose(ps[:, 32 * n:32 * n + NCMP], hidn[:, n // 2, P * (n % 2):P * (n % 2) + P],
                                           ident[0:NCMP, 0:NCMP])
                    ins.then_inc(tp_done, 1)
                elif kind == "CK":
                    pe.wait_ge(small_in, 16 * 5)
                    wait_tp_emptied(pe, ("CX", 0))
                    ps = take_o(it)
                    for hh in range(2):
                        pe.matmul(ps[0:64, 0:NCMP], w2c[:, hh, :], hidc[:, hh, 0:NCMP], start=(hh == 0), stop=(hh == 1))
                    for hh in range(2):
                        ins = pe.matmul(ps[0:NCMP, 64:64 + HD], hidc[:, 2 + hh, 0:NCMP], w2c[:, 2 + hh, :],
                                        start=(hh == 0), stop=(hh == 1))
                    ins.then_inc(o_done, 1)
                elif kind == "CS":
                    wait_emptied(pe, o_free, ("CK", 0), o_act, o_dve)
                    ps = take_sc(it)
                    for i in range(NB):
                        for h in range(NSA_H):
                            c = 32 * (NSA_H * i + h)
                            ins = pe.matmul(ps[:, c:c + 32], nqT[:, h // 2, P * i:P * i + P], kcp[:, h % 2, :],
                                            start=True, stop=True)
                    ins.then_inc(sc_done, 1)
                elif kind == "CT":
                    pe.wait_ge(c_exp, 1)
                    ps = take_tp(it)
                    for i in range(NB):
                        ins = pe.transpose(ps[:, P * i:P * i + P], probc[:, P * i:P * i + P], ident[:, :])
                    ins.then_inc(tp_done, 1)
                elif kind == "CO":
                    wait_tp_emptied(pe, ("CT", 0))
                    for i in range(NB):
                        pe.matmul(take_o(("CO", i))[:, 0:NSA_H * HD], pcT[:, P * i:P * i + P], vbd[:, :], start=True,
                                  stop=True).then_inc(o_done, 1)

            pe.wait_ge(lgT_ready, 1)
            n = NG + NE
            for i in range(NB):
                ins = pe.transpose(bank[3][:, n * i:n * i + n], lgT[:, P * i:P * i + P], ident[0:n, 0:n])
            ins.then_inc(lgT_done, 1)
            pe.wait_ge(sel_ready, 1)
            for i in range(NB):
                for j in range(i + 1):
                    pe.matmul(bank[1][:, NE * i:NE * i + NE], (tri if j == i else ones)[:, :],
                              selb[:, NE * j:NE * j + NE], start=(j == 0), stop=(j == i))
            for j in range(NB):
                ins = pe.matmul(bank[1][:, NB * NE:NB * NE + NE], ones[:, :], selb[:, NE * j:NE * j + NE],
                                start=(j == 0), stop=(j == NB - 1))
            ins.then_inc(pos_mm, 1)
            pe.wait_ge(onehot_ready, 5)
            for n in range(2 * NB):
                for part in range(2):
                    ins = pe.matmul(bank[3][:, 0:NE + NOV], in_lane[:, n, :], part_id[:, part, n, :],
                                    start=(n + part == 0), stop=(n == 2 * NB - 1 and part == 1))
            ins.then_inc(ids_mm, 1)

            def turn_rows(r, i):
                pe.wait_ge(xg_in[r % 2], 16 * (2 * i + r // 2 + 1))
                for half in range(2):
                    use = rows_use(r, i) + half
                    if not (r == 0):
                        pe.wait_ge(e_tp_free, use - 1)
                    for c in range(4):
                        k = 4 * half + c
                        ins = pe.transpose(use_bank(rows_use(r, 0) + half)[:, P * c:P * c + P],
                                           xg[:, r % 2, P * k:P * k + P], ident[:, :])
                    ins.then_inc(e_tp, 1)

            def turn_hidden(r, i):
                pe.wait_ge(hid_done, expert(r, i) + 1)
                pe.wait_ge(e_tp_free, hidden_use(r, i) - 1)
                for c in range(2):
                    ins = pe.transpose(use_bank(3 * r)[:, P * c:P * c + P], hid[:, r % 2, P * c:P * c + P], ident[:, :])
                ins.then_inc(e_tp, 1)

            def gate_up(r, i, k):
                m = pc_mod(r, k)
                pe.wait_ge(e_lo, pc_no(r, i, k) + 1)
                if k == 0:
                    pe.wait_ge(e_tp_free, rows_use(r, i) + 2)
                    if not_before_2(r, i):
                        pe.wait_ge(hid_done, expert(r, i) - 1)
                wh, wl = [t[:, m % MSPLIT, :].rearrange("p (k n) -> p k n", k=2) for t in (m_hi, m_lo)]
                for kk in range(2):
                    c = 2 * k + kk
                    ins = three(bank[r % 2][:, :], xT_hi[:, r % 2, c, :], xT_lo[:, r % 2, c, :], wh[:, kk, :],
                                wl[:, kk, :], c == 0, c == KC - 1)
                ins.then_inc(e_used, 1)

            def down(r, i, k, last=False):
                m = pc_mod(r + 1, 4 + k)
                pe.wait_ge(e_lo, (6 * NE - 2 + k if last else pc_no(r + 1, i, 4 + k)) + 1)
                if k == 0:
                    pe.wait_ge(e_tp_free, hidden_use(r, i) + 1)
                    if not_before_2(r, i):
                        pe.wait_ge(y_done, expert(r, i) - 1)
                for half in range(2):
                    cs = slice(512 * half, 512 * half + 512)
                    ins = three(y_bank(r, half)[:, :], hidT_hi[:, r % 2, k, :], hidT_lo[:, r % 2, k, :],
                                m_hi[:, m % MSPLIT, cs], m_lo[:, m % MSPLIT, cs], k == 0, k == 1)
                ins.then_inc(e_used, 1)

            def pe_opening():
                turn_rows(0, 0)
                for k in range(4):
                    gate_up(0, 0, k)
                turn_rows(1, 0)

            def pe_round(r, i):
                gate_up(r, i, 0)
                gate_up(r, i, 1)
                turn_hidden(r - 1, i)
                gate_up(r, i, 2)
                gate_up(r, i, 3)
                if not is_last(r, i):
                    turn_rows(r + 1, i)
                down(r - 1, i, 0)
                down(r - 1, i, 1)

            rounds(pe, pe_opening, pe_round)
            turn_hidden(3, NE // 4 - 1)
            down(3, NE // 4 - 1, 0, last=True)
            down(3, NE // 4 - 1, 1, last=True)

            pe.wait_ge(ov_ready, 1)
            extra = pe.value_load(ovint[0:1, NOV:NOV + 1], min_val=0, max_val=NOV)
            with pe.If(extra > 0):
                pe.wait_ge(y_done, NE)
                pe.wait_ge(e_tp_free, 3 * NE)
                with pe.Fori(0, NOV) as j:
                    pe.wait_ge(v_gath, 16 * j + 16)
                    for half in range(2):
                        for c in range(4):
                            k = 4 * half + c
                            ins = pe.transpose(tp_bank[half][:, P * c:P * c + P], xg[:, 0, P * k:P * k + P], ident[:, :])
                        ins.then_inc(v_tp, 1)
                    pe.wait_ge(v_xT, 2 * j + 2)
                    pe.wait_ge(v_in, 80 * j + 80)
                    for k in range(KC):
                        ins = pe.matmul(bank[0][:, :], h2T[:, 0, P * k:P * k + P],
                                        mraw[k // 4].rearrange("p (k n) -> p k n", n=2 * EH)[:, k % 4, :],
                                        start=(k == 0), stop=(k == KC - 1))
                    ins.then_inc(v_gu, 1)
                    pe.wait_ge(v_hid, j + 1)
                    for c in range(2):
                        ins = pe.transpose(tp_bank[0][:, P * c:P * c + P], hid[:, 0, P * c:P * c + P], ident[:, :])
                    ins.then_inc(v_htp, 1)
                    pe.wait_ge(v_hT, j + 1)
                    for half in range(2):
                        for k in range(2):
                            ins = pe.matmul(bank[2 + half][:, :], h2T[:, 1, P * k:P * k + P],
                                            mraw[2][:, D * k + 512 * half:D * k + 512 * half + 512],
                                            start=(k == 0), stop=(k == 1))
                        ins.then_inc(v_y, 1)


INPUTS = ["x", "norm_mix_g", "norm_ffn_g", "final_norm_g", "w_in", "b_in", "cmp_w1", "cmp_b1", "cmp_w2", "cmp_pos",
          "w_br_fox", "w_br_nsa", "w_br_moba", "w_out", "w_route_grp", "b_route_grp", "w_route_exp", "b_route_exp",
          "w_exp_gate", "w_exp_up", "w_exp_down"]


def kernel(**inputs):
    import numpy as np
    import concourse.bacc as bacc
    from concourse.bass_utils import run_bass_kernel_spmd

    nc = bacc.Bacc("TRN2", target_bir_lowering=False, num_devices=1)
    arrays, args = {}, []
    for name in INPUTS:
        a = np.ascontiguousarray(inputs[name])
        arrays[f"in_{name}"] = a
        args.append(nc.dram_tensor(f"in_{name}", a.shape, mybir.dt.from_np(a.dtype), kind="ExternalInput").ap())
    args.append(nc.dram_tensor("out", (1, S, D), F32, kind="ExternalOutput").ap())
    build(nc, *args)
    return run_bass_kernel_spmd(nc, [arrays], core_ids=[0]).results[0]["out"]
```
